# Optimizing a Trainium2 kernel written in Bass

```python
import jax, jax.numpy as jnp
from jax import lax
import numpy as np

D_MODEL = 2048
BATCH = 1
SEQ = 256
DEPTH = 2

N_A = DEPTH // 2
N_B = DEPTH - N_A
A_HEADS = 16
Q_LORA = 512
KV_LORA = 512
NOPE_DIM = 128
ROPE_DIM = 64
V_DIM = 128
ROPE_THETA = 10000.0
B_HEADS = 16
B_HEAD_DIM = 128
D_FF = 4 * D_MODEL
Q_BLOCK = 128
NORM_EPS = 1e-6

kernel_name = "yoco_mla_stickbreaking_trunk"

def rms_norm(x, g):
    xf = x.astype(jnp.float32)
    y = xf * lax.rsqrt(jnp.mean(xf * xf, axis=-1, keepdims=True) + NORM_EPS)
    return (y * g.astype(jnp.float32)).astype(x.dtype)

def rope_tables(seq_len):
    pos = jnp.arange(seq_len, dtype=jnp.float32)
    inv_freq = ROPE_THETA ** (-jnp.arange(0, ROPE_DIM, 2, dtype=jnp.float32) / ROPE_DIM)
    ang = pos[:, None] * inv_freq[None, :]
    return jnp.cos(ang), jnp.sin(ang)

def apply_rope(x, cos, sin):
    c = cos[None, :, None, :].astype(x.dtype)
    s = sin[None, :, None, :].astype(x.dtype)
    x1, x2 = x[..., : ROPE_DIM // 2], x[..., ROPE_DIM // 2:]
    return jnp.concatenate([x1 * c - x2 * s, x1 * s + x2 * c], axis=-1)

def causal_softmax_attention(q, k, v, scale):
    bsz, seq, heads, dv = v.shape
    n_blocks = seq // Q_BLOCK
    kpos = jnp.arange(seq)

    def block(i):
        start = i * Q_BLOCK
        qb = lax.dynamic_slice_in_dim(q, start, Q_BLOCK, axis=1)
        s = jnp.einsum('bqhd,bkhd->bhqk', qb, k).astype(jnp.float32) * scale
        qpos = start + jnp.arange(Q_BLOCK)
        mask = kpos[None, :] <= qpos[:, None]
        p = jax.nn.softmax(jnp.where(mask, s, -jnp.inf), axis=-1)
        return jnp.einsum('bhqk,bkhd->bqhd', p.astype(v.dtype), v)

    out = lax.map(block, jnp.arange(n_blocks))
    return out.transpose(1, 0, 2, 3, 4).reshape(bsz, seq, heads, dv)

def stick_breaking_attention(q, k, v, scale):
    bsz, seq, heads, dv = v.shape
    n_blocks = seq // Q_BLOCK
    kpos = jnp.arange(seq)

    def block(i):
        start = i * Q_BLOCK
        qb = lax.dynamic_slice_in_dim(q, start, Q_BLOCK, axis=1)
        z = jnp.einsum('bqhd,bkhd->bhqk', qb, k).astype(jnp.float32) * scale
        qpos = start + jnp.arange(Q_BLOCK)
        strict = kpos[None, :] < qpos[:, None]
        log_beta = jax.nn.log_sigmoid(z)
        log_1m = jnp.where(strict, log_beta - z, 0.0)
        suffix = lax.cumsum(log_1m, axis=3, reverse=True) - log_1m
        a = jnp.where(strict, jnp.exp(log_beta + suffix), 0.0)
        return jnp.einsum('bhqk,bkhd->bqhd', a.astype(v.dtype), v)

    out = lax.map(block, jnp.arange(n_blocks))
    return out.transpose(1, 0, 2, 3, 4).reshape(bsz, seq, heads, dv)

def mla(h, w_dq_dkv, q_norm_g, kv_norm_g, w_uq, w_ukv, w_o, cos, sin):
    bsz, seq, _ = h.shape
    lat = h @ w_dq_dkv
    c_q = lat[..., :Q_LORA]
    c_kv = lat[..., Q_LORA:Q_LORA + KV_LORA]
    k_rope = lat[..., Q_LORA + KV_LORA:]
    q = (rms_norm(c_q, q_norm_g) @ w_uq).reshape(bsz, seq, A_HEADS, NOPE_DIM + ROPE_DIM)
    q = jnp.concatenate([q[..., :NOPE_DIM], apply_rope(q[..., NOPE_DIM:], cos, sin)], axis=-1)
    kv = (rms_norm(c_kv, kv_norm_g) @ w_ukv).reshape(bsz, seq, A_HEADS, NOPE_DIM + V_DIM)
    k_nope, v = kv[..., :NOPE_DIM], kv[..., NOPE_DIM:]
    k_rope = apply_rope(k_rope[:, :, None, :], cos, sin)
    k = jnp.concatenate([k_nope, jnp.broadcast_to(k_rope, (bsz, seq, A_HEADS, ROPE_DIM))], axis=-1)
    o = causal_softmax_attention(q, k, v, (NOPE_DIM + ROPE_DIM) ** -0.5)
    return o.reshape(bsz, seq, A_HEADS * V_DIM) @ w_o

def sq_relu_mlp(h, w_up, w_down):
    return jnp.square(jax.nn.relu(h @ w_up)) @ w_down

def setup_inputs(seed: int = 0) -> dict:
    key = jax.random.key(seed)
    ks = jax.random.split(key, 24)
    f32 = jnp.float32

    def w(k, shape, fan_in):
        return jax.random.normal(k, shape, f32) * (fan_in ** -0.5)

    def gain(k, shape):
        return 1.0 + 0.05 * jax.random.normal(k, shape, f32)

    return {
        "x": jax.random.normal(ks[0], (BATCH, SEQ, D_MODEL), f32),
        "a_pre_g": gain(ks[1], (N_A, D_MODEL)),
        "a_post_g": gain(ks[2], (N_A, D_MODEL)),
        "a_w_dq_dkv": w(ks[3], (N_A, D_MODEL, Q_LORA + KV_LORA + ROPE_DIM), D_MODEL),
        "a_q_norm_g": gain(ks[4], (N_A, Q_LORA)),
        "a_kv_norm_g": gain(ks[5], (N_A, KV_LORA)),
        "a_w_uq": w(ks[6], (N_A, Q_LORA, A_HEADS * (NOPE_DIM + ROPE_DIM)), Q_LORA),
        "a_w_ukv": w(ks[7], (N_A, KV_LORA, A_HEADS * (NOPE_DIM + V_DIM)), KV_LORA),
        "a_w_o": w(ks[8], (N_A, A_HEADS * V_DIM, D_MODEL), A_HEADS * V_DIM),
        "kv_norm_g": gain(ks[9], (D_MODEL,)),
        "w_kv_shared": w(ks[10], (D_MODEL, 2 * B_HEADS * B_HEAD_DIM), D_MODEL),
        "b_pre_g": gain(ks[11], (N_B, D_MODEL)),
        "b_post_g": gain(ks[12], (N_B, D_MODEL)),
        "b_w_q": w(ks[13], (N_B, D_MODEL, B_HEADS * B_HEAD_DIM), D_MODEL),
        "b_w_o": w(ks[14], (N_B, B_HEADS * B_HEAD_DIM, D_MODEL), B_HEADS * B_HEAD_DIM),
        "mlp_pre_g": gain(ks[15], (DEPTH, D_MODEL)),
        "mlp_post_g": gain(ks[16], (DEPTH, D_MODEL)),
        "mlp_w_up": w(ks[17], (DEPTH, D_MODEL, D_FF), D_MODEL),
        "mlp_w_down": w(ks[18], (DEPTH, D_FF, D_MODEL), D_FF),
    }

def reference(x, a_pre_g, a_post_g, a_w_dq_dkv, a_q_norm_g, a_kv_norm_g, a_w_uq, a_w_ukv, a_w_o,
              kv_norm_g, w_kv_shared, b_pre_g, b_post_g, b_w_q, b_w_o,
              mlp_pre_g, mlp_post_g, mlp_w_up, mlp_w_down):
    bsz, seq, _ = x.shape
    cos, sin = rope_tables(seq)
    sb_scale = B_HEAD_DIM ** -0.5
    h = x
    k_sh = v_sh = None
    for layer in range(DEPTH):
        if layer < N_A:
            i = layer
            a = mla(rms_norm(h, a_pre_g[i]), a_w_dq_dkv[i], a_q_norm_g[i], a_kv_norm_g[i],
                    a_w_uq[i], a_w_ukv[i], a_w_o[i], cos, sin)
            h = h + rms_norm(a, a_post_g[i])
        else:
            j = layer - N_A
            q = (rms_norm(h, b_pre_g[j]) @ b_w_q[j]).reshape(bsz, seq, B_HEADS, B_HEAD_DIM)
            o = stick_breaking_attention(q, k_sh, v_sh, sb_scale)
            a = o.reshape(bsz, seq, B_HEADS * B_HEAD_DIM) @ b_w_o[j]
            h = h + rms_norm(a, b_post_g[j])
        m = sq_relu_mlp(rms_norm(h, mlp_pre_g[layer]), mlp_w_up[layer], mlp_w_down[layer])
        h = h + rms_norm(m, mlp_post_g[layer])
        if layer == N_A - 1:
            kv = (rms_norm(h, kv_norm_g) @ w_kv_shared).reshape(bsz, seq, 2, B_HEADS, B_HEAD_DIM)
            k_sh, v_sh = kv[:, :, 0], kv[:, :, 1]
    return h


_drawn_inputs = setup_inputs


def setup_inputs(seed=0):
    import zlib

    import numpy as np

    out = dict(_drawn_inputs(seed))
    spreads = {}
    factors = {'b_pre_g': 6.251}
    for name, (base, spread) in spreads.items():
        noise = np.random.default_rng([zlib.crc32(name.encode()), seed]).standard_normal(out[name].shape)
        drawn = base * np.exp(spread * noise) if base else spread * noise
        out[name] = __import__('jax').numpy.asarray(drawn.astype(out[name].dtype))
    for name, factor in factors.items():
        out[name] = (out[name] * factor).astype(out[name].dtype)
    return out
```

```python
from contextlib import ExitStack

import numpy as np

import concourse.bass as bass
from concourse import mybir

F32 = mybir.dt.float32
F32R = mybir.dt.float32r
ALU = mybir.AluOpType
ACT = mybir.ActivationFunctionType
AX_X = mybir.AxisListType.X

P = 128
SEQ = 256
TB = SEQ // P
D = 2048
KT = D // P
HEADS = 16
NOPE = 128
ROPE = 64
LORA = 512
LT = LORA // P
D_FF = 4 * D
FFN_PARTS = D_FF // D
EPS = 1e-6
MLA_SCALE = float(NOPE + ROPE) ** -0.5
STICK_SCALE = float(P) ** -0.5

NCOL = 512
PIECE = 2 * NCOL
RAW_SLOTS = 4
PIECE_SLOTS = 4
BANKS = 8

UNIT_CHUNKS = (D // NCOL) * (D // (4 * P))
UNIT_PIECES = 2 * UNIT_CHUNKS
GROUP_PIECES = KT // 2
FEATURE_BANKS = D // P
TOKEN_BANKS = (D // NCOL) * TB
TURN_BANKS = KT // 2

STAGES = [
    ("turn_mla", 0, TURN_BANKS),
    ("latents", 2 * 4, 2 * TB),
    ("k_rope", 1, 1),
    ("turn_latents", 0, 2 * LT // 2),
    ("q_mla", HEADS // 2, 3 * HEADS // 2),
    ("kv_mla", HEADS // 2, 4 * HEADS // 2),
    ("mla", 0, 3 * HEADS),
    ("mla_out", UNIT_CHUNKS, TOKEN_BANKS),
    ("turn_mlp0", 0, TURN_BANKS),
    ("mlp0", 2 * UNIT_CHUNKS * FFN_PARTS, (FEATURE_BANKS + TOKEN_BANKS) * FFN_PARTS),
    ("turn_kv", 0, TURN_BANKS),
    ("k_shared", UNIT_CHUNKS, FEATURE_BANKS),
    ("v_shared", UNIT_CHUNKS, TOKEN_BANKS),
    ("turn_q", 0, TURN_BANKS),
    ("q_stick", UNIT_CHUNKS, FEATURE_BANKS),
    ("stick", 0, 2 * HEADS),
    ("stick_out", UNIT_CHUNKS, TOKEN_BANKS),
    ("turn_mlp1", 0, TURN_BANKS),
    ("mlp1", 2 * UNIT_CHUNKS * FFN_PARTS, (FEATURE_BANKS + TOKEN_BANKS) * FFN_PARTS),
]
CHUNK0, BANK0 = {}, {}
_c = _b = 0
for _name, _chunks, _banks in STAGES:
    CHUNK0[_name], BANK0[_name] = _c, _b
    _c, _b = _c + _chunks, _b + _banks
CHUNKS = _c
PIECES = 2 * CHUNKS
BANK_END = {name: BANK0[name] + banks for name, _, banks in STAGES}
MLP_CHUNKS = 2 * UNIT_CHUNKS
MLP_PIECES = 2 * MLP_CHUNKS
MLP_BANKS = FEATURE_BANKS + TOKEN_BANKS
assert MLP_CHUNKS % RAW_SLOTS == 0 and MLP_PIECES % PIECE_SLOTS == 0 and MLP_BANKS % BANKS == 0

USED = []
_used = 0
for _name, _chunks, _banks in STAGES:
    _units = [(2 * _chunks, _banks)]
    if _name.startswith("mlp"):
        _units = [(UNIT_PIECES, FEATURE_BANKS), (UNIT_PIECES, TOKEN_BANKS)] * FFN_PARTS
    _s = BANK0[_name]
    for _pieces, _banks in _units:
        _group = 2 if _name in ("k_rope", "q_mla", "kv_mla") else GROUP_PIECES
        for _p in range(_pieces):
            if _p % _group == _group - 1:
                _s += _banks // (_pieces // _group)
                USED.append(("bank_full", _s))
            else:
                _used += 1
                USED.append(("piece_used", _used))
MLP_USED = MLP_PIECES - MLP_PIECES // GROUP_PIECES
assert len(USED) == PIECES

STAT = {"pre_mla": 0, "latents": 2, "post_mla": 6, "pre_mlp0": 8, "post_mlp0": 10, "pre_kv": 12,
        "post_stick": 14, "pre_mlp1": 16, "post_mlp1": 18}
STATS = 20
NORMED = {"pre_mla": 0, "pre_mlp0": 2, "pre_kv": 4, "pre_q": 6, "pre_mlp1": 8}
RESIDUAL = {"post_mla": 0, "post_mlp0": 2, "post_stick": 4, "post_mlp1": 6}
PRE_GAINS = ["pre_mla", "latents", "pre_mlp0", "pre_kv", "pre_q", "pre_mlp1"]
POST_GAINS = ["post_mla", "post_mlp0", "post_stick", "post_mlp1"]
PRE_GAIN_LOADS = {"pre_mla": 1, "latents": 3, "pre_mlp0": 4, "pre_kv": 5, "pre_q": 6, "pre_mlp1": 7}
POST_GAIN_LOADS = {"post_mla": 1, "post_mlp0": 2, "post_stick": 3, "post_mlp1": 4}

IDENT, CAUSAL, STRICT, SUFFIX, LATER, COS, SIN = 0, 128, 512, 640, 768, 896, 1152
CONST_COLS = 1408

MLA_BANK, STICK_BANK = {}, {}
_n, _m = BANK0["mla"], BANK0["stick"]
for _t in range(HEADS + 2):
    for _what, _lag in (("scores", 0), ("turned", 1), ("out", 2)):
        if 0 <= _t - _lag < HEADS:
            MLA_BANK[_what, _t - _lag] = _n
            _n += 1
    for _what, _lag in (("logits", 1), ("out", 2)):
        if 0 <= _t - _lag < HEADS:
            STICK_BANK[_what, _t - _lag] = _m
            _m += 1


def shape_constants():
    c = np.zeros((P, CONST_COLS), np.float32)
    row, col = np.arange(P)[:, None], np.arange(P)[None, :]
    c[:, IDENT:IDENT + P] = row == col
    tri = np.where(col <= row, 0.0, -1e30)
    c[:, CAUSAL:CAUSAL + P] = tri
    c[:, CAUSAL + 2 * P:CAUSAL + 3 * P] = tri
    c[:, STRICT:STRICT + P] = row < col
    c[:, SUFFIX:SUFFIX + P] = np.where(row >= col, -1.0, 0.0)
    c[:, LATER:LATER + P] = -1.0
    half = ROPE // 2
    inv = np.float32(10000.0) ** (-np.arange(0, ROPE, 2, dtype=np.float32) / np.float32(ROPE))
    ang = (np.arange(SEQ, dtype=np.float32)[:, None] * inv[None, :]).astype(np.float32)
    cos, sin = np.cos(ang).T, np.sin(ang).T
    for q in range(P // half):
        c[q * half:(q + 1) * half, COS:COS + SEQ] = cos
        c[q * half:(q + 1) * half, SIN:SIN + SEQ] = -sin if q % 2 == 0 else sin
    return c


def trunk(nc, x, a_pre_g, a_post_g, w_lat, q_norm_g, kv_norm_g, w_uq, w_ukv, w_mla_o, kv_g, w_kv,
          b_pre_g, b_post_g, w_q, w_stick_o, mlp_pre_g, mlp_post_g, w_up, w_down, consts, out):
    ctx = ExitStack()
    with ctx:
        def sb(name, shape, dt=F32):
            return ctx.enter_context(nc.sbuf_tensor(name, shape, dt))

        def sem(name):
            return ctx.enter_context(nc.semaphore(name))

        resid = sb("resid", [P, TB, D])
        branch = sb("branch", [P, TB, D])
        xT = sb("xT", [P, KT, 2, SEQ], F32R)
        with nc.sbuf_tensor("hidT", [P, KT, 2, SEQ], F32R) as hidT:
            pass
        keyT = sb("keyT", [P, HEADS, SEQ])
        val = sb("val", [P, TB, HEADS * P])
        raw = sb("raw", [P, RAW_SLOTS, 2 * PIECE])
        whi = sb("whi", [P, PIECE_SLOTS, PIECE], F32R)
        wlo = sb("wlo", [P, PIECE_SLOTS, PIECE], F32R)
        gain_pre = sb("gain_pre", [P, D])
        gain_post = sb("gain_post", [P, D])
        with nc.sbuf_tensor("junk", [P, D], F32) as junk:
            pass
        with nc.sbuf_tensor("soft", [P, 4, 384], F32) as soft:
            pass
        qropeT = sb("qropeT", [P, HEADS // 2, SEQ])
        kropeT = sb("kropeT", [P, SEQ])
        work = sb("work", [P, 12, SEQ])
        con = sb("con", [P, CONST_COLS])
        stat = sb("stat", [P, 3, 32])
        power = sb("power", [P, 1])
        rows = sb("rows", [P, 3, 2 * HEADS])
        queryT = branch.rearrange("p b (h t) -> p (b h) t", t=SEQ)
        bank = ctx.enter_context(nc.psum_tensor("bank", [P, BANKS, 512], F32))

        half_sum, full_sum = work[:, 0:4, :], work[:, 4:8, :]
        pairs = work.rearrange("p a t -> p (a t)")
        probs = pairs[:, 0:768].rearrange("p (b n) -> p b n", b=2)
        probsT = pairs[:, 768:1536].rearrange("p (b n) -> p b n", b=2)

        ident = con[:, IDENT:IDENT + P]
        strict2 = con[:, STRICT:STRICT + P].unsqueeze(1).to_broadcast([P, 2, P])

        raw_loaded = [sem(f"raw_loaded{i}") for i in range(RAW_SLOTS)]
        hi_ready, lo_ready, piece_used = sem("hi_ready"), sem("lo_ready"), sem("piece_used")
        bank_full, bank_free = sem("bank_full"), sem("bank_free")
        x_loaded, con_loaded, out_stored = sem("x_loaded"), sem("con_loaded"), sem("out_stored")
        pre_gain_loaded, post_gain_loaded = sem("pre_gain_loaded"), sem("post_gain_loaded")
        power_set, branch_zeroed = sem("power_set"), sem("branch_zeroed")
        squares_ready, mean_ready, rms_ready = sem("squares_ready"), sem("mean_ready"), sem("rms_ready")
        branch_scaled, resid_ready = sem("branch_scaled"), sem("resid_ready")
        normed_ready, latent_normed, turned_hi = sem("normed_ready"), sem("latent_normed"), sem("turned_hi")
        half_ready, relu2_ready = sem("half_ready"), sem("relu2_ready")
        hidden_hi, hidden_ready = sem("hidden_hi"), sem("hidden_ready")
        swapped, rope_terms, rope_ready = sem("swapped"), sem("rope_terms"), sem("rope_ready")
        row_max, exp_ready, sum_inverse = sem("row_max"), sem("exp_ready"), sem("sum_inverse")
        probs_ready, out_hi = sem("probs_ready"), sem("out_hi")
        logit_ready, abs_ready, exp_abs, log_term = sem("logit_ready"), sem("abs_ready"), sem("exp_abs"), sem("log_term")
        softplus, masked_softplus = sem("softplus"), sem("masked_softplus")
        stick_exp, stick_ready = sem("stick_exp"), sem("stick_ready")

        def bank_of(s):
            return bank[:, s % BANKS, :]

        def split_moves(p):
            q = p % PIECE_SLOTS
            if p // 2 == CHUNK0["k_rope"]:
                src = raw[:, (p // 2) % RAW_SLOTS, (p % 2) * NCOL:(p % 2 + 1) * NCOL]
                src = src.rearrange("p (k n) -> p k n", n=ROPE)
                hi, lo = (w[:, q, :].rearrange("p (k d n) -> p k d n", d=2, n=ROPE) for w in (whi, wlo))
                return [(src, hi[:, :, d, :], lo[:, :, d, :]) for d in range(2)]
            if CHUNK0["q_mla"] <= p // 2 < CHUNK0["kv_mla"]:
                n = 2 * 2 * (NOPE + ROPE)
                src = raw[:, (p // 2) % RAW_SLOTS, (p % 2) * n:(p % 2 + 1) * n]
                src = src.rearrange("p (k h n) -> p k h n", k=2, h=2)
                hi, lo = (w[:, q, 0:n].rearrange("p (k n) -> p k n", k=2) for w in (whi, wlo))
                out = []
                for c0, c1, d0 in ((0, NOPE, 0), (NOPE, NOPE + ROPE, 2 * NOPE)):
                    d1 = d0 + 2 * (c1 - c0)
                    out.append((src[:, :, :, c0:c1], *(w[:, :, d0:d1].rearrange("p k (h n) -> p k h n", h=2)
                                                       for w in (hi, lo))))
                return out
            return [(raw[:, (p // 2) % RAW_SLOTS, (p % 2) * PIECE:(p % 2 + 1) * PIECE], whi[:, q, :], wlo[:, q, :])]

        HALF = {"k_rope": 0, "q_mla": 1, "kv_mla": 1 + 3 * HEADS // 2}
        HALF["mlp0"] = HALF["kv_mla"] + HEADS
        HALF["k_shared"] = HALF["mlp0"] + FEATURE_BANKS * FFN_PARTS
        HALF["q_stick"] = HALF["k_shared"] + FEATURE_BANKS
        HALF["mlp1"] = HALF["q_stick"] + FEATURE_BANKS
        HIDDEN = {"mlp0": 0, "mlp1": FEATURE_BANKS * FFN_PARTS}
        TURN, n = {}, 0
        for name, _, banks in STAGES:
            if name.startswith("turn"):
                TURN[name], n = n, n + banks
        ZEROED = {"mlp0": 1, "mlp1": 2}

        block = ctx.enter_context(nc.Block())

        @block.sync
        def _(sp):
            def load_chunk(c, off, dst, src):
                if c >= RAW_SLOTS:
                    sp.wait_ge(lo_ready, 2 * (c - RAW_SLOTS) + 2 + off * 2)
                sp.dma_start(dst, src).then_inc(raw_loaded[c % RAW_SLOTS], 16)

            def raw_chunk(c, k, n):
                return raw[:, c % RAW_SLOTS, 0:k * n].rearrange("p (k n) -> p k n", k=k)

            def load_unit(c0, off, w, row0, col0):
                wv = w.rearrange("(k p) n -> p k n", p=P)
                for i in range(UNIT_CHUNKS):
                    g, kc = divmod(i, KT // 4)
                    load_chunk(c0 + i, off, raw_chunk(c0 + i, 4, NCOL),
                               wv[:, bass.ds(row0 + 4 * kc, 4), bass.ds(col0 + g * NCOL, NCOL)])

            sp.dma_start(con[:, :], consts).then_inc(con_loaded, 16)
            for b in range(TB):
                sp.dma_start(resid[:, b, :], x[0, b * P:(b + 1) * P, :]).then_inc(x_loaded, 16)
                sp.wait_ge(x_loaded, 16 * (b + 1))
            c = CHUNK0["latents"]
            wv = w_lat[0].rearrange("(k p) n -> p k n", p=P)
            for i in range(8):
                g, kc = divmod(i, 4)
                load_chunk(c + i, 0, raw_chunk(c + i, 4, NCOL),
                           wv[:, 4 * kc:4 * kc + 4, g * NCOL:(g + 1) * NCOL])
            c = CHUNK0["k_rope"]
            load_chunk(c, 0, raw_chunk(c, KT, ROPE), wv[:, :, 2 * LORA:2 * LORA + ROPE])
            c = CHUNK0["q_mla"]
            wv = w_uq[0].rearrange("(k p) n -> p k n", p=P)
            for i in range(HEADS // 2):
                n2 = 2 * (NOPE + ROPE)
                load_chunk(c + i, 0, raw_chunk(c + i, LT, n2), wv[:, :, i * n2:(i + 1) * n2])
            c = CHUNK0["kv_mla"]
            wv = w_ukv[0].rearrange("(k p) n -> p k n", p=P)
            for i in range(HEADS // 2):
                load_chunk(c + i, 0, raw_chunk(c + i, LT, NCOL), wv[:, :, i * NCOL:(i + 1) * NCOL])
            load_unit(CHUNK0["mla_out"], 0, w_mla_o[0], 0, 0)

            def load_mlp(name, layer):
                with sp.Fori(0, FFN_PARTS) as part:
                    c0 = CHUNK0[name]
                    load_unit(c0, part * MLP_CHUNKS, w_up[layer], 0, part * D)
                    load_unit(c0 + UNIT_CHUNKS, part * MLP_CHUNKS, w_down[layer], part * KT, 0)

            load_mlp("mlp0", 0)
            load_unit(CHUNK0["k_shared"], 0, w_kv, 0, 0)
            load_unit(CHUNK0["v_shared"], 0, w_kv, 0, D)
            load_unit(CHUNK0["q_stick"], 0, w_q[0], 0, 0)
            load_unit(CHUNK0["stick_out"], 0, w_stick_o[0], 0, 0)
            load_mlp("mlp1", 1)
            for b in range(TB):
                sp.wait_ge(resid_ready, RESIDUAL["post_mlp1"] + b + 1)
                sp.dma_start(out[0, b * P:(b + 1) * P, :], resid[:, b, :]).then_inc(out_stored, 16)
            sp.wait_ge(out_stored, 16 * TB)

        @block.gpsimd
        def _(pool):
            def load_gain(tile, g, loaded):
                pool.dma_start(tile, g.partition_broadcast(P)).then_inc(loaded, 16)

            def inverse_rms(name, count, width):
                for i in range(STAT[name], STAT[name] + count):
                    pool.wait_ge(squares_ready, i + 1)
                    nc.gpsimd.tensor_scalar(stat[:, 1, i:i + 1], stat[:, 0, i:i + 1], 1.0 / width, EPS,
                                            ALU.mult, ALU.add).then_inc(mean_ready, 1)
                    pool.wait_ge(mean_ready, i + 1)
                    nc.gpsimd.tensor_tensor(stat[:, 2, i:i + 1], stat[:, 1, i:i + 1], power[:, :],
                                            ALU.pow).then_inc(rms_ready, 1)

            load_gain(gain_pre[:, :], a_pre_g[0], pre_gain_loaded)
            load_gain(gain_post[:, :], a_post_g[0], post_gain_loaded)
            nc.gpsimd.memset(power[:, :], -0.5).then_inc(power_set, 1)
            pool.wait_ge(power_set, 1)
            inverse_rms("pre_mla", TB, D)
            pool.wait_ge(normed_ready, NORMED["pre_mla"] + TB)
            pool.wait_ge(pre_gain_loaded, 16)
            load_gain(gain_pre[:, 0:LORA], q_norm_g[0], pre_gain_loaded)
            load_gain(gain_pre[:, LORA:2 * LORA], kv_norm_g[0], pre_gain_loaded)
            inverse_rms("latents", 2 * TB, LORA)
            pool.wait_ge(latent_normed, 2 * TB)
            load_gain(gain_pre[:, :], mlp_pre_g[0], pre_gain_loaded)

            def zero_branch(turned):
                pool.wait_ge(bank_free, BANK_END[turned])
                nc.gpsimd.memset(branch[:, :, :], 0.0).then_inc(branch_zeroed, 1)

            inverse_rms("post_mla", TB, D)
            inverse_rms("pre_mlp0", TB, D)
            pool.wait_ge(resid_ready, RESIDUAL["post_mla"] + TB)
            load_gain(gain_post[:, :], mlp_post_g[0], post_gain_loaded)
            pool.wait_ge(normed_ready, NORMED["pre_mlp0"] + TB)
            load_gain(gain_pre[:, :], kv_g, pre_gain_loaded)
            zero_branch("turn_mlp0")
            inverse_rms("post_mlp0", TB, D)
            inverse_rms("pre_kv", TB, D)
            pool.wait_ge(resid_ready, RESIDUAL["post_mlp0"] + TB)
            load_gain(gain_post[:, :], b_post_g[0], post_gain_loaded)
            pool.wait_ge(normed_ready, NORMED["pre_kv"] + TB)
            load_gain(gain_pre[:, :], b_pre_g[0], pre_gain_loaded)
            pool.wait_ge(normed_ready, NORMED["pre_q"] + TB)
            load_gain(gain_pre[:, :], mlp_pre_g[1], pre_gain_loaded)
            for t in range(HEADS):
                pool.wait_ge(stick_exp, t + 1)
                diag = probs[:, t % 2, :].rearrange("p (b n) -> p b n", b=3)[:, 0:3:2, :]
                nc.gpsimd.tensor_tensor(diag, diag, strict2, ALU.mult).then_inc(stick_ready, 1)
            inverse_rms("post_stick", TB, D)
            inverse_rms("pre_mlp1", TB, D)
            pool.wait_ge(resid_ready, RESIDUAL["post_stick"] + TB)
            load_gain(gain_post[:, :], mlp_post_g[1], post_gain_loaded)
            zero_branch("turn_mlp1")
            inverse_rms("post_mlp1", TB, D)

        @block.scalar
        def _(act):
            def split_hi(p, part=0):
                if p % 2 == 0:
                    c = p // 2
                    act.wait_ge(raw_loaded[c % RAW_SLOTS],
                                16 * (c // RAW_SLOTS + 1) + part * (16 * MLP_CHUNKS // RAW_SLOTS))
                moves = split_moves(p)
                for src, hi, lo in moves[:-1]:
                    nc.scalar.activation(hi, src, ACT.Copy)
                src, hi, lo = moves[-1]
                nc.scalar.activation(hi, src, ACT.Copy).then_inc(hi_ready, 1)

            def split_ahead(p, part=0):
                if p + PIECE_SLOTS < PIECES:
                    signal, value = USED[p]
                    if signal == "bank_full":
                        act.wait_ge(bank_full, value + part * MLP_BANKS)
                    else:
                        act.wait_ge(piece_used, value + part * MLP_USED)
                    split_hi(p + PIECE_SLOTS, part)

            def squares(name, b, src):
                i = STAT[name] + b
                if i:
                    act.wait_ge(squares_ready, i)
                nc.scalar.activation(junk[:, 0:src.shape[-1]], src, ACT.Square,
                                     accum_out=stat[:, 0, i:i + 1]).then_inc(squares_ready, 1)

            def turn_hi(name, k0, dst=xT):
                for i in range(BANK_END[name] - BANK0[name]):
                    s = BANK0[name] + i
                    act.wait_ge(bank_full, s + 1)
                    nc.scalar.activation(dst[:, k0 + 2 * i:k0 + 2 * i + 2, 0, :],
                                         bank_of(s).rearrange("p (k t) -> p k t", k=2),
                                         ACT.Copy).then_inc(turned_hi, 1)

            def take_half(s, off, i, scale=1.0, before=None):
                if before is not None:
                    act.wait_ge(bank_free, before + 1)
                act.wait_ge(bank_full, s + 1 + off)
                nc.scalar.activation(half_sum[:, i % 4, :], bank_of(s)[:, SEQ:2 * SEQ], ACT.Copy,
                                     scale=scale).then_inc(half_ready, 1)

            def swap_rope(s, n):
                act.wait_ge(bank_free, s + 1)
                for q in range(4):
                    src = full_sum[32 * (q ^ 1):32 * (q ^ 1) + 32, 0, :]
                    nc.scalar.activation(full_sum[32 * q:32 * q + 32, 1, :], src, ACT.Copy).then_inc(swapped, 1)

            def feature_stage(name, scale):
                for i in range(UNIT_PIECES):
                    if i % GROUP_PIECES == GROUP_PIECES - 1:
                        for f in range(4):
                            s = BANK0[name] + i // GROUP_PIECES * 4 + f
                            take_half(s, 0, f, scale, before=s - 4 if i >= GROUP_PIECES else None)
                    split_ahead(2 * CHUNK0[name] + i)

            def token_stage(name):
                for i in range(UNIT_PIECES):
                    split_ahead(2 * CHUNK0[name] + i)

            def post_norm(name):
                for b in range(TB):
                    squares(name, b, branch[:, b, :])

            def pre_norm(name, post):
                for b in range(TB):
                    act.wait_ge(resid_ready, RESIDUAL[post] + b + 1)
                    squares(name, b, resid[:, b, :])

            for p in range(PIECE_SLOTS):
                split_hi(p)
            for b in range(TB):
                act.wait_ge(x_loaded, 16 * (b + 1))
                squares("pre_mla", b, resid[:, b, :])
            turn_hi("turn_mla", 0)
            for i in range(2 * (CHUNK0["k_rope"] - CHUNK0["latents"])):
                split_ahead(2 * CHUNK0["latents"] + i)
            for b in range(TB):
                for part in range(2):
                    act.wait_ge(bank_free, BANK0["latents"] + TB * part + b + 1)
                    squares("latents", 2 * b + part, branch[:, b, part * LORA:(part + 1) * LORA])
            take_half(BANK0["k_rope"], 0, 0)
            swap_rope(BANK0["k_rope"], 0)
            for i in range(2):
                split_ahead(2 * CHUNK0["k_rope"] + i)
            turn_hi("turn_latents", KT - 2 * LT)
            for i in range(HEADS // 2):
                s = BANK0["q_mla"] + 3 * i
                for f in range(3):
                    take_half(s + f, 0, f, MLA_SCALE, before=s + f - 3 if i else None)
                swap_rope(s + 2, 1 + i)
                for j in range(2):
                    split_ahead(2 * (CHUNK0["q_mla"] + i) + j)
            for i in range(HEADS // 2):
                s = BANK0["kv_mla"] + 4 * i
                for f in range(2):
                    take_half(s + f, 0, f, before=s + f - 4 if i else None)
                for j in range(2):
                    split_ahead(2 * (CHUNK0["kv_mla"] + i) + j)

            def out_split(t, s):
                act.wait_ge(bank_full, s + 1)
                nc.scalar.activation(xT[:, t, 0, :], bank_of(s)[:, 0:SEQ], ACT.Copy).then_inc(out_hi, 1)

            for step in range(HEADS + 2):
                if step < HEADS:
                    t = step
                    act.wait_ge(row_max, 2 * t + 2)
                    for q, (c0, c1) in enumerate(((0, P), (P, 3 * P))):
                        i = 2 * t + q
                        nc.scalar.activation(probs[:, t % 2, c0:c1], probs[:, t % 2, c0:c1], ACT.Exp,
                                             bias=rows[:, 0, i:i + 1],
                                             accum_out=rows[:, 1, i:i + 1]).then_inc(exp_ready, 1)
                if step >= 2:
                    out_split(step - 2, MLA_BANK["out", step - 2])
                if step < HEADS:
                    act.wait_ge(sum_inverse, t + 1)
                    for q, (c0, c1) in enumerate(((0, P), (P, 3 * P))):
                        i = 2 * t + q
                        nc.scalar.activation(probs[:, t % 2, c0:c1], probs[:, t % 2, c0:c1], ACT.Copy,
                                             scale=rows[:, 2, i:i + 1]).then_inc(probs_ready, 1)
            token_stage("mla_out")
            act.wait_ge(bank_free, BANK_END["mla_out"])
            post_norm("post_mla")
            pre_norm("pre_mlp0", "post_mla")
            turn_hi("turn_mlp0", 0)

            def mlp_part(name, part, last=False):
                p0, s0 = 2 * CHUNK0[name], BANK0[name]
                soff, foff = part * MLP_BANKS, part * FEATURE_BANKS
                for i in range(UNIT_PIECES):
                    if i % GROUP_PIECES == GROUP_PIECES - 1:
                        g = i // GROUP_PIECES
                        for f in range(5):
                            if f < 4:
                                take_half(s0 + 4 * g + f, soff, f)
                            if f >= 1:
                                k = 4 * g + f - 1
                                act.wait_ge(relu2_ready, HIDDEN[name] + k + 1 + foff)
                                nc.scalar.activation(hidT[:, k, 0, :], full_sum[:, k % 4, :],
                                                     ACT.Copy).then_inc(hidden_hi, 1)
                    split_ahead(p0 + i, part)
                for i in range(UNIT_PIECES):
                    if not (last and i >= UNIT_PIECES - PIECE_SLOTS):
                        split_ahead(p0 + UNIT_PIECES + i, part)

            with act.Fori(0, FFN_PARTS) as part:
                mlp_part("mlp0", part)
            act.wait_ge(bank_free, BANK_END["mlp0"])
            post_norm("post_mlp0")
            pre_norm("pre_kv", "post_mlp0")
            turn_hi("turn_kv", 0)

            feature_stage("k_shared", 1.0)
            token_stage("v_shared")
            turn_hi("turn_q", 0)
            feature_stage("q_stick", STICK_SCALE)
            for step in range(HEADS + 2):
                if step < HEADS:
                    t = step
                    s = STICK_BANK["logits", t]
                    tail = soft[:, t % 2, :]
                    act.wait_ge(logit_ready, t + 1)
                    nc.scalar.activation(tail, bank_of(s)[:, 0:384], ACT.Abs).then_inc(abs_ready, 1)
                    act.wait_ge(abs_ready, t + 1)
                    nc.scalar.activation(tail, tail, ACT.Exp, scale=-1.0).then_inc(exp_abs, 1)
                    act.wait_ge(exp_abs, t + 1)
                    nc.scalar.activation(tail, tail, ACT.Ln, bias=1.0).then_inc(log_term, 1)
                if 1 <= step <= HEADS:
                    t = step - 1
                    act.wait_ge(bank_free, STICK_BANK["logits", t] + 1)
                    nc.scalar.activation(probs[:, t % 2, :], probs[:, t % 2, :], ACT.Exp).then_inc(stick_exp, 1)
                if step >= 2:
                    out_split(step - 2, STICK_BANK["out", step - 2])
            token_stage("stick_out")
            act.wait_ge(bank_free, BANK_END["stick_out"])
            post_norm("post_stick")
            pre_norm("pre_mlp1", "post_stick")
            turn_hi("turn_mlp1", 0)
            with act.Fori(0, FFN_PARTS - 1) as part:
                mlp_part("mlp1", part)
            mlp_part("mlp1", FFN_PARTS - 1, last=True)
            act.wait_ge(bank_free, BANK_END["mlp1"])
            post_norm("post_mlp1")

        @block.tensor
        def _(pe):
            def open_bank(s, off=0):
                if s >= BANKS:
                    pe.wait_ge(bank_free, s - BANKS + 1 + off)

            def piece(p, off=0, k=2):
                pe.wait_ge(lo_ready, p + 1 + off)
                n = 2 * (NOPE + ROPE) if CHUNK0["q_mla"] <= p // 2 < CHUNK0["kv_mla"] else PIECE // k
                return [w[:, p % PIECE_SLOTS, 0:k * n].rearrange("p (k n) -> p k n", k=k) for w in (whi, wlo)]

            def feature_block(s, hi, lo, op, first, last):
                nc.tensor.matmul(bank_of(s), hi, op, start=first, stop=False)
                return nc.tensor.matmul(bank_of(s)[:, 0:SEQ], lo, op[:, 0, :], start=False, stop=last)

            def token_block(dst, hi, lo, op, b, first, last):
                t = slice(b * P, (b + 1) * P)
                nc.tensor.matmul(dst, op[:, 0, t], hi, start=first, stop=False)
                nc.tensor.matmul(dst, op[:, 0, t], lo, start=False, stop=False)
                return nc.tensor.matmul(dst, op[:, 1, t], hi, start=False, stop=last)

            def feature_unit(p0, s0, poff=0, soff=0, op=xT, ready=None):
                for i in range(UNIT_PIECES):
                    g, kp = divmod(i, GROUP_PIECES)
                    if ready and g == 0:
                        ready(kp)
                    hi, lo = piece(p0 + i, poff)
                    for f in range(4):
                        s = s0 + 4 * g + f
                        if kp == 0:
                            open_bank(s, soff)
                        for k in range(2):
                            kt = 2 * kp + k
                            mm = feature_block(s, hi[:, k, f * P:(f + 1) * P], lo[:, k, f * P:(f + 1) * P],
                                               op[:, kt, :, :], kt == 0, kt == KT - 1)
                        if kp == GROUP_PIECES - 1:
                            mm.then_inc(bank_full, 1)
                    if kp < GROUP_PIECES - 1:
                        mm.then_inc(piece_used, 1)

            def token_unit(p0, s0, poff=0, soff=0, op=xT, groups=D // NCOL, ready=None):
                for i in range(groups * GROUP_PIECES):
                    g, kp = divmod(i, GROUP_PIECES)
                    if ready and g == 0:
                        ready(kp)
                    hi, lo = piece(p0 + i, poff)
                    for b in range(TB):
                        s = s0 + TB * g + b
                        if kp == 0:
                            open_bank(s, soff)
                        for k in range(2):
                            kt = 2 * kp + k
                            mm = token_block(bank_of(s), hi[:, k, :], lo[:, k, :], op[:, kt, :, :], b,
                                             kt == 0, kt == KT - 1)
                        if kp == GROUP_PIECES - 1:
                            mm.then_inc(bank_full, 1)
                    if kp < GROUP_PIECES - 1:
                        mm.then_inc(piece_used, 1)

            def turn(name, tiles):
                for i in range(tiles // 2):
                    s = BANK0[name] + i
                    open_bank(s)
                    for j in range(4):
                        kt, b = 2 * i + j // 2, j % 2
                        mm = nc.tensor.transpose(bank_of(s)[:, j * P:(j + 1) * P],
                                                 branch[:, b, kt * P:(kt + 1) * P], ident)
                    mm.then_inc(bank_full, 1)

            def turned(name):
                return lambda kp: pe.wait_ge(bank_free, BANK0[name] + kp + 1)

            pe.wait_ge(con_loaded, 16)
            pe.wait_ge(normed_ready, NORMED["pre_mla"] + TB)
            turn("turn_mla", KT)
            token_unit(2 * CHUNK0["latents"], BANK0["latents"], groups=2, ready=turned("turn_mla"))
            s = BANK0["k_rope"]
            open_bank(s)
            for i in range(2):
                hi, lo = piece(2 * CHUNK0["k_rope"] + i, k=KT // 2)
                for k in range(KT // 2):
                    kt = i * KT // 2 + k
                    mm = feature_block(s, hi[:, k, :], lo[:, k, :], xT[:, kt, :, :], kt == 0, kt == KT - 1)
                mm.then_inc(piece_used if i == 0 else bank_full, 1)
            pe.wait_ge(latent_normed, 2 * TB)
            turn("turn_latents", 2 * LT)
            cq, ckv = KT - 2 * LT, KT - LT
            for i in range(HEADS // 2):
                s = BANK0["q_mla"] + 3 * i
                for j in range(2):
                    if i == 0:
                        pe.wait_ge(bank_free, BANK0["turn_latents"] + j + 1)
                    hi, lo = piece(2 * (CHUNK0["q_mla"] + i) + j)
                    for f in range(3):
                        if j == 0:
                            open_bank(s + f)
                        for k in range(2):
                            kt = 2 * j + k
                            cols = slice(f * P, (f + 1) * P)
                            mm = feature_block(s + f, hi[:, k, cols], lo[:, k, cols], xT[:, cq + kt, :, :], kt == 0, kt == LT - 1)
                        if j == 1:
                            mm.then_inc(bank_full, 1)
                    if j == 0:
                        mm.then_inc(piece_used, 1)
            for i in range(HEADS // 2):
                s = BANK0["kv_mla"] + 4 * i
                for j in range(2):
                    if i == 0:
                        pe.wait_ge(bank_free, BANK0["turn_latents"] + 2 + j + 1)
                    hi, lo = piece(2 * (CHUNK0["kv_mla"] + i) + j)
                    for f in range(2):
                        if j == 0:
                            open_bank(s + f)
                        for k in range(2):
                            kt = 2 * j + k
                            cols = slice(2 * f * P, (2 * f + 1) * P)
                            mm = feature_block(s + f, hi[:, k, cols], lo[:, k, cols], xT[:, ckv + kt, :, :],
                                               kt == 0, kt == LT - 1)
                        if j == 1:
                            mm.then_inc(bank_full, 1)
                    for b in range(TB):
                        if j == 0:
                            open_bank(s + 2 + b)
                        dst = bank_of(s + 2 + b)[:, 0:2 * P]
                        for k in range(2):
                            kt = 2 * j + k
                            h, l = (w[:, k, :].rearrange("p (h n) -> p h n", n=P)[:, 1:4:2, :] for w in (hi, lo))
                            mm = token_block(dst, h, l, xT[:, ckv + kt, :, :], b, kt == 0, kt == LT - 1)
                        if j == 1:
                            mm.then_inc(bank_full, 1)
                    if j == 0:
                        mm.then_inc(piece_used, 1)

            def weighted_values(t, s, w):
                h = slice(t * P, (t + 1) * P)
                open_bank(s)
                nc.tensor.matmul(bank_of(s)[:, 0:SEQ], val[:, 0, h], w[:, 0:SEQ], start=True, stop=False)
                nc.tensor.matmul(bank_of(s)[:, P:SEQ], val[:, 1, h], w[:, SEQ:3 * P], start=False,
                                 stop=True).then_inc(bank_full, 1)

            pe.wait_ge(bank_free, BANK_END["kv_mla"])
            pe.wait_ge(rope_ready, 1 + HEADS // 2)
            for step in range(HEADS + 2):
                if step < HEADS:
                    t = step
                    s = MLA_BANK["scores", t]
                    open_bank(s)
                    r = slice(ROPE * (t % 2), ROPE * (t % 2) + ROPE)
                    for q, (c0, keys) in enumerate(((0, P), (P, 2 * P))):
                        qs = slice(q * P, (q + 1) * P)
                        dst = bank_of(s)[:, c0:c0 + keys]
                        nc.tensor.matmul(dst, queryT[:, t, qs], keyT[:, t, 0:keys], start=True, stop=False)
                        mm = nc.tensor.matmul(dst, qropeT[r, t // 2, qs], kropeT[r, 0:keys], start=False, stop=True)
                    mm.then_inc(bank_full, 1)
                if 1 <= step <= HEADS:
                    t = step - 1
                    s = MLA_BANK["turned", t]
                    open_bank(s)
                    pe.wait_ge(probs_ready, 2 * t + 2)
                    for j in range(3):
                        mm = nc.tensor.transpose(bank_of(s)[:, j * P:(j + 1) * P],
                                                 probs[:, t % 2, j * P:(j + 1) * P], ident)
                    mm.then_inc(bank_full, 1)
                if step >= 2:
                    t = step - 2
                    pe.wait_ge(bank_free, MLA_BANK["turned", t] + 1)
                    weighted_values(t, MLA_BANK["out", t], probsT[:, t % 2, :])
            pe.wait_ge(bank_free, BANK_END["mla"])
            token_unit(2 * CHUNK0["mla_out"], BANK0["mla_out"])

            def mlp(name, turn_name, loop_parts):
                pe.wait_ge(normed_ready, NORMED[turn_name] + TB)
                turn("turn_" + name, KT)
                pe.wait_ge(bank_free, BANK_END["turn_" + name])

                def one(part):
                    poff, soff, foff = part * MLP_PIECES, part * MLP_BANKS, part * FEATURE_BANKS
                    feature_unit(2 * CHUNK0[name], BANK0[name], poff, soff)

                    def hidden(kp):
                        pe.wait_ge(hidden_ready, HIDDEN[name] + 2 * kp + 2 + foff)

                    token_unit(2 * CHUNK0[name] + UNIT_PIECES, BANK0[name] + FEATURE_BANKS, poff, soff,
                               op=hidT, ready=hidden)

                with pe.Fori(0, FFN_PARTS) as part:
                    one(part)

            mlp("mlp0", "pre_mlp0", FFN_PARTS)
            pe.wait_ge(normed_ready, NORMED["pre_kv"] + TB)
            turn("turn_kv", KT)
            feature_unit(2 * CHUNK0["k_shared"], BANK0["k_shared"], ready=turned("turn_kv"))
            token_unit(2 * CHUNK0["v_shared"], BANK0["v_shared"])
            pe.wait_ge(normed_ready, NORMED["pre_q"] + TB)
            turn("turn_q", KT)
            feature_unit(2 * CHUNK0["q_stick"], BANK0["q_stick"], ready=turned("turn_q"))

            pe.wait_ge(bank_free, BANK_END["q_stick"])
            suffix, later = con[:, SUFFIX:SUFFIX + P], con[:, LATER:LATER + P]
            for step in range(HEADS + 2):
                if step < HEADS:
                    t = step
                    s = STICK_BANK["logits", t]
                    open_bank(s)
                    z = bank_of(s)
                    nc.tensor.matmul(z[:, 0:SEQ], keyT[:, t, 0:P], queryT[:, t, :], start=True, stop=False,
                                     skip_group_check=True)
                    nc.tensor.matmul(z[:, SEQ:3 * P], keyT[:, t, P:SEQ], queryT[:, t, P:SEQ], start=False,
                                     stop=False, skip_group_check=True).then_inc(logit_ready, 1)
                if 1 <= step <= HEADS:
                    t = step - 1
                    z, sp_ = bank_of(STICK_BANK["logits", t]), soft[:, 2 + t % 2, :]
                    pe.wait_ge(masked_softplus, t + 1)
                    nc.tensor.matmul(z[:, 0:SEQ], suffix, sp_[:, 0:SEQ], start=False, stop=False,
                                     skip_group_check=True)
                    nc.tensor.matmul(z[:, P:SEQ], later, sp_[:, SEQ:3 * P], start=False, stop=False,
                                     skip_group_check=True)
                    nc.tensor.matmul(z[:, SEQ:3 * P], suffix, sp_[:, SEQ:3 * P], start=False, stop=True,
                                     skip_group_check=True).then_inc(bank_full, 1)
                if step >= 2:
                    t = step - 2
                    pe.wait_ge(stick_ready, t + 1)
                    weighted_values(t, STICK_BANK["out", t], probs[:, t % 2, :])
            pe.wait_ge(bank_free, BANK_END["stick"])
            token_unit(2 * CHUNK0["stick_out"], BANK0["stick_out"])
            mlp("mlp1", "pre_mlp1", FFN_PARTS)

        @block.vector
        def _(dve):
            def split_lo(p, part=0):
                dve.wait_ge(hi_ready, p + 1 + part * MLP_PIECES)
                moves = split_moves(p)
                for src, hi, lo in moves[:-1]:
                    nc.vector.tensor_tensor(lo, src, hi.bitcast(F32), ALU.subtract)
                src, hi, lo = moves[-1]
                nc.vector.tensor_tensor(lo, src, hi.bitcast(F32), ALU.subtract).then_inc(lo_ready, 1)

            def split_ahead(p, part=0):
                if p + PIECE_SLOTS < PIECES:
                    split_lo(p + PIECE_SLOTS, part)

            def add_halves(dst, s, off, i, half, scale=1.0):
                dve.wait_ge(half_ready, half + 1)
                nc.vector.scalar_tensor_tensor(out=dst, in0=bank_of(s)[:, 0:SEQ], scalar=scale,
                                               in1=half_sum[:, i % 4, :], op0=ALU.mult,
                                               op1=ALU.add).then_inc(bank_free, 1)

            def rotate(dst, s, n):
                dve.wait_ge(swapped, 4 * (n + 1))
                for i, table in ((0, COS), (1, SIN)):
                    nc.vector.tensor_tensor(full_sum[:, i, :], full_sum[:, i, :], con[:, table:table + SEQ],
                                            ALU.mult).then_inc(rope_terms, 1)
                dve.wait_ge(rope_terms, 2 * (n + 1))
                nc.vector.tensor_tensor(dst, full_sum[:, 0, :], full_sum[:, 1, :], ALU.add).then_inc(rope_ready, 1)

            def norm_rows(name, load, normed):
                dve.wait_ge(pre_gain_loaded, 16 * PRE_GAIN_LOADS[load])
                for b in range(TB):
                    i = STAT[name] + b
                    dve.wait_ge(rms_ready, i + 1)
                    nc.vector.scalar_tensor_tensor(out=branch[:, b, :], in0=resid[:, b, :],
                                                   scalar=stat[:, 2, i:i + 1], in1=gain_pre[:, :],
                                                   op0=ALU.mult, op1=ALU.mult).then_inc(normed_ready, 1)

            def add_branch(name):
                dve.wait_ge(post_gain_loaded, 16 * POST_GAIN_LOADS[name])
                for b in range(TB):
                    i = STAT[name] + b
                    dve.wait_ge(rms_ready, i + 1)
                    nc.vector.scalar_tensor_tensor(out=branch[:, b, :], in0=branch[:, b, :],
                                                   scalar=stat[:, 2, i:i + 1], in1=gain_post[:, :],
                                                   op0=ALU.mult, op1=ALU.mult).then_inc(branch_scaled, 1)
                    dve.wait_ge(branch_scaled, RESIDUAL[name] + b + 1)
                    nc.vector.tensor_tensor(resid[:, b, :], resid[:, b, :], branch[:, b, :],
                                            ALU.add).then_inc(resid_ready, 1)

            def turn_lo(name, k0):
                for i in range(BANK_END[name] - BANK0[name]):
                    s = BANK0[name] + i
                    dve.wait_ge(turned_hi, TURN[name] + i + 1)
                    k = slice(k0 + 2 * i, k0 + 2 * i + 2)
                    nc.vector.tensor_tensor(xT[:, k, 1, :], bank_of(s).rearrange("p (k t) -> p k t", k=2),
                                            xT[:, k, 0, :].bitcast(F32), ALU.subtract).then_inc(bank_free, 1)

            def feature_stage(name, dst, scale=1.0):
                for i in range(UNIT_PIECES):
                    if i % GROUP_PIECES == GROUP_PIECES - 1:
                        for f in range(4):
                            k = i // GROUP_PIECES * 4 + f
                            add_halves(dst[:, k, :], BANK0[name] + k, 0, f, HALF[name] + k, scale)
                    split_ahead(2 * CHUNK0[name] + i)

            def token_stage(name, dst, groups=D // NCOL):
                for i in range(groups * GROUP_PIECES):
                    if i % GROUP_PIECES == GROUP_PIECES - 1:
                        g = i // GROUP_PIECES
                        for b in range(TB):
                            s = BANK0[name] + TB * g + b
                            dve.wait_ge(bank_full, s + 1)
                            nc.vector.tensor_copy(dst[:, b, g * NCOL:(g + 1) * NCOL],
                                                  bank_of(s)).then_inc(bank_free, 1)
                    split_ahead(2 * CHUNK0[name] + i)

            for p in range(PIECE_SLOTS):
                split_lo(p)
            dve.wait_ge(x_loaded, 16 * TB)
            norm_rows("pre_mla", "pre_mla", 0)
            turn_lo("turn_mla", 0)
            token_stage("latents", branch, groups=2)
            dve.wait_ge(con_loaded, 16)
            add_halves(full_sum[:, 0, :], BANK0["k_rope"], 0, 0, HALF["k_rope"])
            rotate(kropeT[:, :], BANK0["k_rope"], 0)
            dve.wait_ge(pre_gain_loaded, 16 * PRE_GAIN_LOADS["latents"])
            for b in range(TB):
                for part in range(2):
                    i = STAT["latents"] + 2 * b + part
                    c = branch[:, b, part * LORA:(part + 1) * LORA]
                    dve.wait_ge(rms_ready, i + 1)
                    nc.vector.scalar_tensor_tensor(out=c, in0=c, scalar=stat[:, 2, i:i + 1],
                                                   in1=gain_pre[:, part * LORA:(part + 1) * LORA],
                                                   op0=ALU.mult, op1=ALU.mult).then_inc(latent_normed, 1)
            for i in range(2):
                split_ahead(2 * CHUNK0["k_rope"] + i)
            turn_lo("turn_latents", KT - 2 * LT)
            for i in range(HEADS // 2):
                s, h = BANK0["q_mla"] + 3 * i, HALF["q_mla"] + 3 * i
                for f in range(2):
                    add_halves(queryT[:, 2 * i + f, :], s + f, 0, f, h + f, MLA_SCALE)
                dve.wait_ge(rope_ready, 1 + i)
                add_halves(full_sum[:, 0, :], s + 2, 0, 2, h + 2, MLA_SCALE)
                rotate(qropeT[:, i, :], s + 2, 1 + i)
                for j in range(2):
                    split_ahead(2 * (CHUNK0["q_mla"] + i) + j)
            for i in range(HEADS // 2):
                s, h = BANK0["kv_mla"] + 4 * i, HALF["kv_mla"] + 2 * i
                for f in range(2):
                    add_halves(keyT[:, 2 * i + f, :], s + f, 0, f, h + f)
                for b in range(TB):
                    dve.wait_ge(bank_full, s + 3 + b)
                    nc.vector.tensor_copy(val[:, b, 2 * i * P:2 * (i + 1) * P],
                                          bank_of(s + 2 + b)[:, 0:2 * P]).then_inc(bank_free, 1)
                for j in range(2):
                    split_ahead(2 * (CHUNK0["kv_mla"] + i) + j)

            def out_rest(t, s, n):
                dve.wait_ge(out_hi, n + 1)
                nc.vector.tensor_tensor(xT[:, t, 1, :], bank_of(s)[:, 0:SEQ], xT[:, t, 0, :].bitcast(F32),
                                        ALU.subtract).then_inc(bank_free, 1)

            for step in range(HEADS + 2):
                if step < HEADS:
                    t = step
                    s = MLA_BANK["scores", t]
                    pr = probs[:, t % 2, :]
                    dve.wait_ge(bank_full, s + 1)
                    nc.vector.tensor_tensor(pr, bank_of(s)[:, 0:3 * P], con[:, CAUSAL:CAUSAL + 3 * P],
                                            ALU.add).then_inc(bank_free, 1)
                    dve.wait_ge(bank_free, s + 1)
                    for q, (c0, c1) in enumerate(((0, P), (P, 3 * P))):
                        nc.vector.tensor_reduce(rows[:, 0, 2 * t + q:2 * t + q + 1], pr[:, c0:c1], AX_X,
                                                ALU.max, negate=True).then_inc(row_max, 1)
                if 1 <= step <= HEADS:
                    t = step - 1
                    s = MLA_BANK["turned", t]
                    dve.wait_ge(bank_full, s + 1)
                    nc.vector.tensor_copy(probsT[:, t % 2, :], bank_of(s)[:, 0:3 * P]).then_inc(bank_free, 1)
                if step >= 2:
                    out_rest(step - 2, MLA_BANK["out", step - 2], step - 2)
                if step < HEADS:
                    t = step
                    dve.wait_ge(exp_ready, 2 * t + 2)
                    nc.vector.reciprocal(rows[:, 2, 2 * t:2 * t + 2],
                                         rows[:, 1, 2 * t:2 * t + 2]).then_inc(sum_inverse, 1)
            token_stage("mla_out", branch)
            add_branch("post_mla")
            norm_rows("pre_mlp0", "pre_mlp0", 1)
            turn_lo("turn_mlp0", 0)

            def mlp_part(name, part, last=False):
                p0, s0 = 2 * CHUNK0[name], BANK0[name]
                soff, foff = part * MLP_BANKS, part * FEATURE_BANKS
                for i in range(UNIT_PIECES):
                    if i % GROUP_PIECES == GROUP_PIECES - 1:
                        g = i // GROUP_PIECES
                        for f in range(5):
                            if f < 4:
                                k = 4 * g + f
                                v = full_sum[:, f, :]
                                if k >= 4:
                                    dve.wait_ge(hidden_ready, HIDDEN[name] + k - 3 + foff)
                                add_halves(v, s0 + k, soff, f, HALF[name] + k + foff)
                                dve.wait_ge(bank_free, s0 + k + 1 + soff)
                                nc.vector.scalar_tensor_tensor(out=v, in0=v, scalar=0.0, in1=v, op0=ALU.max,
                                                               op1=ALU.mult).then_inc(relu2_ready, 1)
                            if f >= 1:
                                k = 4 * g + f - 1
                                dve.wait_ge(hidden_hi, HIDDEN[name] + k + 1 + foff)
                                nc.vector.tensor_tensor(hidT[:, k, 1, :], full_sum[:, f - 1, :],
                                                        hidT[:, k, 0, :].bitcast(F32),
                                                        ALU.subtract).then_inc(hidden_ready, 1)
                    split_ahead(p0 + i, part)
                for i in range(UNIT_PIECES):
                    if i % GROUP_PIECES == GROUP_PIECES - 1:
                        g = i // GROUP_PIECES
                        for b in range(TB):
                            s = s0 + FEATURE_BANKS + TB * g + b
                            dst = branch[:, b, g * NCOL:(g + 1) * NCOL]
                            dve.wait_ge(bank_full, s + 1 + soff)
                            nc.vector.tensor_tensor(dst, bank_of(s), dst, ALU.add).then_inc(bank_free, 1)
                    if not (last and i >= UNIT_PIECES - PIECE_SLOTS):
                        split_ahead(p0 + UNIT_PIECES + i, part)

            dve.wait_ge(branch_zeroed, ZEROED["mlp0"])
            with dve.Fori(0, FFN_PARTS) as part:
                mlp_part("mlp0", part)
            add_branch("post_mlp0")
            norm_rows("pre_kv", "pre_kv", 2)
            turn_lo("turn_kv", 0)
            feature_stage("k_shared", keyT)
            token_stage("v_shared", val)
            norm_rows("pre_kv", "pre_q", 3)
            turn_lo("turn_q", 0)
            feature_stage("q_stick", queryT, STICK_SCALE)

            for step in range(HEADS + 2):
                if step < HEADS:
                    t = step
                    s = STICK_BANK["logits", t]
                    spt = soft[:, 2 + t % 2, :]
                    dve.wait_ge(log_term, t + 1)
                    nc.vector.scalar_tensor_tensor(out=spt, in0=bank_of(s)[:, 0:3 * P], scalar=0.0,
                                                   in1=soft[:, t % 2, :], op0=ALU.max,
                                                   op1=ALU.add).then_inc(softplus, 1)
                    diag = spt.rearrange("p (b n) -> p b n", b=3)[:, 0:3:2, :]
                    dve.wait_ge(softplus, t + 1)
                    nc.vector.tensor_tensor(diag, diag, strict2, ALU.mult).then_inc(masked_softplus, 1)
                if 1 <= step <= HEADS:
                    t = step - 1
                    s = STICK_BANK["logits", t]
                    dve.wait_ge(bank_full, s + 1)
                    nc.vector.tensor_scalar(probs[:, t % 2, :], bank_of(s)[:, 0:3 * P], 0.0, None,
                                            ALU.min).then_inc(bank_free, 1)
                if step >= 2:
                    out_rest(step - 2, STICK_BANK["out", step - 2], HEADS + step - 2)
            token_stage("stick_out", branch)
            add_branch("post_stick")
            norm_rows("pre_mlp1", "pre_mlp1", 4)
            turn_lo("turn_mlp1", 0)
            dve.wait_ge(branch_zeroed, ZEROED["mlp1"])
            with dve.Fori(0, FFN_PARTS - 1) as part:
                mlp_part("mlp1", part)
            mlp_part("mlp1", FFN_PARTS - 1, last=True)
            add_branch("post_mlp1")


_INS = ["x", "a_pre_g", "a_post_g", "a_w_dq_dkv", "a_q_norm_g", "a_kv_norm_g", "a_w_uq", "a_w_ukv",
        "a_w_o", "kv_norm_g", "w_kv_shared", "b_pre_g", "b_post_g", "b_w_q", "b_w_o", "mlp_pre_g",
        "mlp_post_g", "mlp_w_up", "mlp_w_down"]


def kernel(**inputs):
    import concourse.bacc as _bacc
    from concourse.bass_utils import run_bass_kernel_spmd as _run

    nc = _bacc.Bacc("TRN2", target_bir_lowering=False, num_devices=1)
    arrays, args = {}, []
    for name in _INS:
        a = np.ascontiguousarray(inputs[name])
        arrays[f"in_{name}"] = a
        args.append(nc.dram_tensor(f"in_{name}", a.shape, mybir.dt.from_np(a.dtype), kind="ExternalInput").ap())
    c = shape_constants()
    arrays["shape_constants"] = c
    args.append(nc.dram_tensor("shape_constants", c.shape, F32, kind="ExternalInput").ap())
    args.append(nc.dram_tensor("out", (1, SEQ, D), F32, kind="ExternalOutput").ap())
    trunk(nc, *args)
    r = _run(nc, [arrays], core_ids=[0])
    return r.results[0]["out"]
```

```python
from contextlib import ExitStack

import numpy as np

import concourse.bass as bass
from concourse import mybir

F32 = mybir.dt.float32
F32R = mybir.dt.float32r
ALU = mybir.AluOpType
ACT = mybir.ActivationFunctionType
AX_X = mybir.AxisListType.X

P = 128
SEQ = 256
TB = SEQ // P
D = 2048
KT = D // P
HEADS = 16
NOPE = 128
ROPE = 64
LORA = 512
LT = LORA // P
D_FF = 4 * D
FFN_PARTS = D_FF // D
EPS = 1e-6
MLA_SCALE = float(NOPE + ROPE) ** -0.5
STICK_SCALE = float(P) ** -0.5

NCOL = 512
PIECE = 2 * NCOL
RAW_SLOTS = 4
PIECE_SLOTS = 4
BANKS = 8

UNIT_CHUNKS = (D // NCOL) * (D // (4 * P))
UNIT_PIECES = 2 * UNIT_CHUNKS
GROUP_PIECES = KT // 2
FEATURE_BANKS = D // P
TOKEN_BANKS = (D // NCOL) * TB
TURN_BANKS = KT // 2

STAGES = [
    ("turn_mla", 0, TURN_BANKS),
    ("latents", 2 * 4, 2 * TB),
    ("k_rope", 1, 1),
    ("turn_latents", 0, 2 * LT // 2),
    ("q_mla", HEADS // 2, 3 * HEADS // 2),
    ("kv_mla", HEADS // 2, 4 * HEADS // 2),
    ("mla", 0, 3 * HEADS),
    ("mla_out", UNIT_CHUNKS, TOKEN_BANKS),
    ("turn_mlp0", 0, TURN_BANKS),
    ("mlp0", 2 * UNIT_CHUNKS * FFN_PARTS, (FEATURE_BANKS + TOKEN_BANKS) * FFN_PARTS),
    ("turn_kv", 0, TURN_BANKS),
    ("k_shared", UNIT_CHUNKS, FEATURE_BANKS),
    ("v_shared", UNIT_CHUNKS, TOKEN_BANKS),
    ("turn_q", 0, TURN_BANKS),
    ("q_stick", UNIT_CHUNKS, FEATURE_BANKS),
    ("stick", 0, 2 * HEADS),
    ("stick_out", UNIT_CHUNKS, TOKEN_BANKS),
    ("turn_mlp1", 0, TURN_BANKS),
    ("mlp1", 2 * UNIT_CHUNKS * FFN_PARTS, (FEATURE_BANKS + TOKEN_BANKS) * FFN_PARTS),
]
CHUNK0, BANK0 = {}, {}
_c = _b = 0
for _name, _chunks, _banks in STAGES:
    CHUNK0[_name], BANK0[_name] = _c, _b
    _c, _b = _c + _chunks, _b + _banks
CHUNKS = _c
PIECES = 2 * CHUNKS
BANK_END = {name: BANK0[name] + banks for name, _, banks in STAGES}
MLP_CHUNKS = 2 * UNIT_CHUNKS
MLP_PIECES = 2 * MLP_CHUNKS
MLP_BANKS = FEATURE_BANKS + TOKEN_BANKS
assert MLP_CHUNKS % RAW_SLOTS == 0 and MLP_PIECES % PIECE_SLOTS == 0 and MLP_BANKS % BANKS == 0

USED = []
_used = 0
for _name, _chunks, _banks in STAGES:
    _units = [(2 * _chunks, _banks)]
    if _name.startswith("mlp"):
        _units = [(UNIT_PIECES, FEATURE_BANKS), (UNIT_PIECES, TOKEN_BANKS)] * FFN_PARTS
    _s = BANK0[_name]
    for _pieces, _banks in _units:
        _group = 2 if _name in ("k_rope", "q_mla", "kv_mla") else GROUP_PIECES
        for _p in range(_pieces):
            if _p % _group == _group - 1:
                _s += _banks // (_pieces // _group)
                USED.append(("bank_full", _s))
            else:
                _used += 1
                USED.append(("piece_used", _used))
MLP_USED = MLP_PIECES - MLP_PIECES // GROUP_PIECES
assert len(USED) == PIECES

NORMS = [("pre_mla", 0, 1, 2), ("pre_mla", 1, 1, 2), ("latents", None, 2 * TB, 1)]
for _post, _pre in (("post_mla", "pre_mlp0"), ("post_mlp0", "pre_kv"), ("post_stick", "pre_mlp1"),
                    ("post_mlp1", None)):
    NORMS.append((_post, None, TB, D // NCOL))
    if _pre:
        NORMS += [(_pre, b, 1, 2) for b in range(TB)]
REQUEST, STAT, SQUARES = {}, {}, {}
_col = _part = 0
for _i, (_name, _b, _cols, _parts) in enumerate(NORMS):
    REQUEST[_name, _b], STAT[_name, _b], SQUARES[_name, _b] = _i, _col, _part
    _col, _part = _col + _cols, _part + _cols * _parts
STATS = _col
QUARTERS = D // NCOL
NORMED = {n: i * QUARTERS * TB for i, n in enumerate(["pre_mla", "pre_mlp0", "pre_kv", "pre_q", "pre_mlp1"])}
RESIDUAL = {n: i * 2 * TB for i, n in enumerate(["post_mla", "post_mlp0", "post_stick", "post_mlp1"])}
GAINED = {n: i * (QUARTERS - 1) * TB for i, n in enumerate(["post_mla", "post_mlp0", "post_stick", "post_mlp1"])}
PRE_GAINS = ["pre_mla", "latents", "pre_mlp0", "pre_kv", "pre_q", "pre_mlp1"]
POST_GAINS = ["post_mla", "post_mlp0", "post_stick", "post_mlp1"]
PRE_GAIN_LOADS = {"pre_mla": 1, "latents": 3, "pre_mlp0": 4, "pre_kv": 5, "pre_q": 6, "pre_mlp1": 7}
POST_GAIN_LOADS = {"post_mla": 1, "post_mlp0": 2, "post_stick": 3, "post_mlp1": 4}

IDENT, CAUSAL, STRICT, SUFFIX, LATER, COS, SIN = 0, 128, 512, 640, 768, 896, 1152
CONST_COLS = 1408

MLA_BANK, STICK_BANK = {}, {}
_n, _m = BANK0["mla"], BANK0["stick"]
for _t in range(HEADS + 2):
    for _what, _lag in (("scores", 0), ("out", 2), ("turned", 1)):
        if 0 <= _t - _lag < HEADS:
            MLA_BANK[_what, _t - _lag] = _n
            _n += 1
    for _what, _lag in (("logits", 1), ("out", 2)):
        if 0 <= _t - _lag < HEADS:
            STICK_BANK[_what, _t - _lag] = _m
            _m += 1

BANK_ID = [s % BANKS for s in range(sum(banks for _, _, banks in STAGES))]
for _name, _next in (("mla", "mla_out"), ("stick", "stick_out")):
    for _s in range(BANK0[_name], BANK_END[_name]):
        BANK_ID[_s] = (BANK0[_next] + TB + (_s - BANK0[_name]) % (BANKS - TB)) % BANKS
BEFORE, _last = [], {}
for _s, _id in enumerate(BANK_ID):
    BEFORE.append(_last.get(_id))
    _last[_id] = _s
FILL_LAG = 4
FILLED = (HEADS + 2 - FILL_LAG) // 2
assert FILLED < GROUP_PIECES


def shape_constants():
    c = np.zeros((P, CONST_COLS), np.float32)
    row, col = np.arange(P)[:, None], np.arange(P)[None, :]
    c[:, IDENT:IDENT + P] = row == col
    tri = np.where(col <= row, 0.0, -1e30)
    c[:, CAUSAL:CAUSAL + P] = tri
    c[:, CAUSAL + 2 * P:CAUSAL + 3 * P] = tri
    c[:, STRICT:STRICT + P] = row < col
    c[:, SUFFIX:SUFFIX + P] = np.where(row >= col, -1.0, 0.0)
    c[:, LATER:LATER + P] = -1.0
    half = ROPE // 2
    inv = np.float32(10000.0) ** (-np.arange(0, ROPE, 2, dtype=np.float32) / np.float32(ROPE))
    ang = (np.arange(SEQ, dtype=np.float32)[:, None] * inv[None, :]).astype(np.float32)
    cos, sin = np.cos(ang).T, np.sin(ang).T
    for q in range(P // half):
        c[q * half:(q + 1) * half, COS:COS + SEQ] = cos
        c[q * half:(q + 1) * half, SIN:SIN + SEQ] = -sin if q % 2 == 0 else sin
    return c


def trunk(nc, x, a_pre_g, a_post_g, w_lat, q_norm_g, kv_norm_g, w_uq, w_ukv, w_mla_o, kv_g, w_kv,
          b_pre_g, b_post_g, w_q, w_stick_o, mlp_pre_g, mlp_post_g, w_up, w_down, consts, out):
    ctx = ExitStack()
    with ctx:
        def sb(name, shape, dt=F32):
            return ctx.enter_context(nc.sbuf_tensor(name, shape, dt))

        def sem(name):
            return ctx.enter_context(nc.semaphore(name))

        resid = sb("resid", [P, TB, D])
        branch = sb("branch", [P, TB, D])
        xT = sb("xT", [P, KT, 2, SEQ], F32R)
        with nc.sbuf_tensor("hidT", [P, KT, 2, SEQ], F32R) as hidT:
            pass
        keyT = sb("keyT", [P, HEADS, SEQ])
        val = sb("val", [P, TB, HEADS * P])
        raw = sb("raw", [P, RAW_SLOTS, 2 * PIECE])
        whi = sb("whi", [P, PIECE_SLOTS, PIECE], F32R)
        wlo = sb("wlo", [P, PIECE_SLOTS, PIECE], F32R)
        gain_pre = sb("gain_pre", [P, D])
        gain_post = sb("gain_post", [P, D])
        with nc.sbuf_tensor("junk", [P, D], F32) as junk:
            pass
        with nc.sbuf_tensor("soft", [P, 4, 384], F32) as soft:
            pass
        qropeT = sb("qropeT", [P, HEADS // 2, SEQ])
        kropeT = sb("kropeT", [P, SEQ])
        work = sb("work", [P, 12, SEQ])
        con = sb("con", [P, CONST_COLS])
        squares = sb("squares", [P, STATS, QUARTERS])
        stat = sb("stat", [P, 3, STATS])
        power = sb("power", [P, 2 * TB])
        rows = sb("rows", [P, 3, 2 * HEADS])
        queryT = branch.rearrange("p b (h t) -> p (b h) t", t=SEQ)
        bank = ctx.enter_context(nc.psum_tensor("bank", [P, BANKS, 512], F32))

        half_sum, full_sum = work[:, 0:4, :], work[:, 4:8, :]
        pairs = work.rearrange("p a t -> p (a t)")
        probs = pairs[:, 0:768].rearrange("p (b n) -> p b n", b=2)
        probsT = pairs[:, 768:1536].rearrange("p (b n) -> p b n", b=2)

        ident = con[:, IDENT:IDENT + P]
        strict2 = con[:, STRICT:STRICT + P].unsqueeze(1).to_broadcast([P, 2, P])

        raw_loaded = [sem(f"raw_loaded{i}") for i in range(RAW_SLOTS)]
        hi_ready, lo_ready, piece_used = sem("hi_ready"), sem("lo_ready"), sem("piece_used")
        bank_full, bank_free = sem("bank_full"), sem("bank_free")
        x_loaded = [sem(f"x_loaded{b}") for b in range(TB)]
        con_loaded, out_stored = sem("con_loaded"), sem("out_stored")
        pre_gain_loaded, post_gain_loaded = sem("pre_gain_loaded"), sem("post_gain_loaded")
        power_set, branch_zeroed = sem("power_set"), sem("branch_zeroed")
        squares_ready, sum_ready = sem("squares_ready"), sem("sum_ready")
        mean_ready, rms_ready = sem("mean_ready"), sem("rms_ready")
        gain_scaled, last_scaled, resid_ready = sem("gain_scaled"), sem("last_scaled"), sem("resid_ready")
        normed_ready, latent_normed, turned_hi = sem("normed_ready"), sem("latent_normed"), sem("turned_hi")
        half_ready, relu2_ready = sem("half_ready"), sem("relu2_ready")
        hidden_hi, hidden_ready = sem("hidden_hi"), sem("hidden_ready")
        swapped_low, swapped_high = sem("swapped_low"), sem("swapped_high")
        rope_terms, rope_ready = sem("rope_terms"), sem("rope_ready")
        row_max, exp_ready, sum_inverse = sem("row_max"), sem("exp_ready"), sem("sum_inverse")
        probs_ready, out_hi = sem("probs_ready"), sem("out_hi")
        logit_ready, abs_ready, exp_abs, log_term = sem("logit_ready"), sem("abs_ready"), sem("exp_abs"), sem("log_term")
        softplus, masked_softplus = sem("softplus"), sem("masked_softplus")
        stick_exp, stick_ready = sem("stick_exp"), sem("stick_ready")

        def bank_of(s):
            return bank[:, BANK_ID[s], :]

        def split_moves(p):
            q = p % PIECE_SLOTS
            if p // 2 == CHUNK0["k_rope"]:
                src = raw[:, (p // 2) % RAW_SLOTS, (p % 2) * NCOL:(p % 2 + 1) * NCOL]
                src = src.rearrange("p (k n) -> p k n", n=ROPE)
                hi, lo = (w[:, q, :].rearrange("p (k d n) -> p k d n", d=2, n=ROPE) for w in (whi, wlo))
                return [(src, hi[:, :, d, :], lo[:, :, d, :]) for d in range(2)]
            if CHUNK0["q_mla"] <= p // 2 < CHUNK0["kv_mla"]:
                n = 2 * 2 * (NOPE + ROPE)
                src = raw[:, (p // 2) % RAW_SLOTS, (p % 2) * n:(p % 2 + 1) * n]
                src = src.rearrange("p (k h n) -> p k h n", k=2, h=2)
                hi, lo = (w[:, q, 0:n].rearrange("p (k n) -> p k n", k=2) for w in (whi, wlo))
                out = []
                for c0, c1, d0 in ((0, NOPE, 0), (NOPE, NOPE + ROPE, 2 * NOPE)):
                    d1 = d0 + 2 * (c1 - c0)
                    out.append((src[:, :, :, c0:c1], *(w[:, :, d0:d1].rearrange("p k (h n) -> p k h n", h=2)
                                                       for w in (hi, lo))))
                return out
            return [(raw[:, (p // 2) % RAW_SLOTS, (p % 2) * PIECE:(p % 2 + 1) * PIECE], whi[:, q, :], wlo[:, q, :])]

        HALF = {"k_rope": 0, "q_mla": 1, "kv_mla": 1 + 3 * HEADS // 2}
        HALF["mlp0"] = HALF["kv_mla"] + HEADS
        HALF["k_shared"] = HALF["mlp0"] + FEATURE_BANKS * FFN_PARTS
        HALF["q_stick"] = HALF["k_shared"] + FEATURE_BANKS
        HALF["mlp1"] = HALF["q_stick"] + FEATURE_BANKS
        HIDDEN = {"mlp0": 0, "mlp1": FEATURE_BANKS * FFN_PARTS}
        TURN, n = {}, 0
        for name, _, banks in STAGES:
            if name.startswith("turn"):
                TURN[name], n = n, n + banks
        ZEROED = {"mlp0": 1, "mlp1": 2}
        BRANCH_BANK = {"post_mla": BANK0["mla_out"], "post_mlp0": BANK_END["mlp0"] - TOKEN_BANKS,
                       "post_stick": BANK0["stick_out"], "post_mlp1": BANK_END["mlp1"] - TOKEN_BANKS}

        block = ctx.enter_context(nc.Block())

        @block.sync
        def _(sp):
            def load_chunk(c, off, dst, src):
                if c >= RAW_SLOTS:
                    sp.wait_ge(lo_ready, 2 * (c - RAW_SLOTS) + 2 + off * 2)
                sp.dma_start(dst, src).then_inc(raw_loaded[c % RAW_SLOTS], 16)

            def raw_chunk(c, k, n):
                return raw[:, c % RAW_SLOTS, 0:k * n].rearrange("p (k n) -> p k n", k=k)

            def load_unit(c0, off, w, row0, col0):
                wv = w.rearrange("(k p) n -> p k n", p=P)
                for i in range(UNIT_CHUNKS):
                    g, kc = divmod(i, KT // 4)
                    load_chunk(c0 + i, off, raw_chunk(c0 + i, 4, NCOL),
                               wv[:, bass.ds(row0 + 4 * kc, 4), bass.ds(col0 + g * NCOL, NCOL)])

            for b in range(TB):
                sp.dma_start(resid[:, b, :], x[0, b * P:(b + 1) * P, :]).then_inc(x_loaded[b], 16)
            sp.dma_start(con[:, :], consts).then_inc(con_loaded, 16)
            c = CHUNK0["latents"]
            wv = w_lat[0].rearrange("(k p) n -> p k n", p=P)
            for i in range(8):
                g, kc = divmod(i, 4)
                load_chunk(c + i, 0, raw_chunk(c + i, 4, NCOL),
                           wv[:, 4 * kc:4 * kc + 4, g * NCOL:(g + 1) * NCOL])
            c = CHUNK0["k_rope"]
            load_chunk(c, 0, raw_chunk(c, KT, ROPE), wv[:, :, 2 * LORA:2 * LORA + ROPE])
            c = CHUNK0["q_mla"]
            wv = w_uq[0].rearrange("(k p) n -> p k n", p=P)
            for i in range(HEADS // 2):
                n2 = 2 * (NOPE + ROPE)
                load_chunk(c + i, 0, raw_chunk(c + i, LT, n2), wv[:, :, i * n2:(i + 1) * n2])
            c = CHUNK0["kv_mla"]
            wv = w_ukv[0].rearrange("(k p) n -> p k n", p=P)
            for i in range(HEADS // 2):
                load_chunk(c + i, 0, raw_chunk(c + i, LT, NCOL), wv[:, :, i * NCOL:(i + 1) * NCOL])
            load_unit(CHUNK0["mla_out"], 0, w_mla_o[0], 0, 0)

            def load_mlp(name, layer):
                with sp.Fori(0, FFN_PARTS) as part:
                    c0 = CHUNK0[name]
                    load_unit(c0, part * MLP_CHUNKS, w_up[layer], 0, part * D)
                    load_unit(c0 + UNIT_CHUNKS, part * MLP_CHUNKS, w_down[layer], part * KT, 0)

            load_mlp("mlp0", 0)
            load_unit(CHUNK0["k_shared"], 0, w_kv, 0, 0)
            load_unit(CHUNK0["v_shared"], 0, w_kv, 0, D)
            load_unit(CHUNK0["q_stick"], 0, w_q[0], 0, 0)
            load_unit(CHUNK0["stick_out"], 0, w_stick_o[0], 0, 0)
            load_mlp("mlp1", 1)
            for b in range(TB):
                for h in range(2):
                    cols = slice(h * D // 2, (h + 1) * D // 2)
                    sp.wait_ge(resid_ready, RESIDUAL["post_mlp1"] + 2 * b + h + 1)
                    sp.dma_start(out[0, b * P:(b + 1) * P, cols], resid[:, b, cols]).then_inc(out_stored, 16)
            sp.wait_ge(out_stored, 16 * 2 * TB)

        @block.gpsimd
        def _(pool):
            def load_gain(tile, g, loaded):
                pool.dma_start(tile, g.partition_broadcast(P)).then_inc(loaded, 16)

            def inverse_rms(name, width, blocks=(None,)):
                for b in blocks:
                    r, i = REQUEST[name, b], STAT[name, b]
                    cols = slice(i, i + NORMS[r][2])
                    pool.wait_ge(sum_ready, r + 1)
                    nc.gpsimd.tensor_scalar(stat[:, 1, cols], stat[:, 0, cols], 1.0 / width, EPS,
                                            ALU.mult, ALU.add).then_inc(mean_ready, 1)
                    pool.wait_ge(mean_ready, r + 1)
                    nc.gpsimd.tensor_tensor(stat[:, 2, cols], stat[:, 1, cols],
                                            power[:, 0:NORMS[r][2]], ALU.pow).then_inc(rms_ready, 1)

            def scale_by_gain(name):
                pool.wait_ge(post_gain_loaded, 16 * POST_GAIN_LOADS[name])
                for g in range(QUARTERS - 1):
                    for b in range(TB):
                        cols = slice(g * NCOL, (g + 1) * NCOL)
                        pool.wait_ge(squares_ready, SQUARES[name, None] + TB * g + b + 1)
                        nc.gpsimd.tensor_tensor(branch[:, b, cols], branch[:, b, cols], gain_post[:, cols],
                                                ALU.mult).then_inc(gain_scaled, 1)

            def zero_branch(turned):
                pool.wait_ge(bank_free, BANK_END[turned])
                nc.gpsimd.memset(branch[:, :, :], 0.0).then_inc(branch_zeroed, 1)

            def rotate(dst, s, n):
                u, w = full_sum[:, 2 * (n % 2), :], full_sum[:, 2 * (n % 2) + 1, :]
                pool.wait_ge(bank_free, s + 1)
                nc.gpsimd.tensor_tensor(dst, u, con[:, COS:COS + SEQ], ALU.mult).then_inc(rope_terms, 1)
                pool.wait_ge(swapped_low, 2 * (n + 1))
                pool.wait_ge(swapped_high, 2 * (n + 1))
                nc.gpsimd.tensor_tensor(w, w, con[:, SIN:SIN + SEQ], ALU.mult).then_inc(rope_terms, 1)
                pool.wait_ge(rope_terms, 2 * (n + 1))
                nc.gpsimd.tensor_tensor(dst, dst, w, ALU.add).then_inc(rope_ready, 1)

            all_normed = QUARTERS * TB
            load_gain(gain_pre[:, :], a_pre_g[0], pre_gain_loaded)
            nc.gpsimd.memset(power[:, :], -0.5).then_inc(power_set, 1)
            pool.wait_ge(power_set, 1)
            inverse_rms("pre_mla", D, range(TB))
            pool.wait_ge(normed_ready, NORMED["pre_mla"] + all_normed)
            load_gain(gain_post[:, :], a_post_g[0], post_gain_loaded)
            load_gain(gain_pre[:, 0:LORA], q_norm_g[0], pre_gain_loaded)
            load_gain(gain_pre[:, LORA:2 * LORA], kv_norm_g[0], pre_gain_loaded)
            pool.wait_ge(con_loaded, 16)
            rotate(kropeT[:, :], BANK0["k_rope"], 0)
            inverse_rms("latents", LORA)
            pool.wait_ge(latent_normed, 2 * TB)
            load_gain(gain_pre[:, :], mlp_pre_g[0], pre_gain_loaded)
            for i in range(HEADS // 2):
                rotate(qropeT[:, i, :], BANK0["q_mla"] + 3 * i + 2, 1 + i)
            scale_by_gain("post_mla")
            inverse_rms("post_mla", D)
            inverse_rms("pre_mlp0", D, range(TB))
            load_gain(gain_post[:, :], mlp_post_g[0], post_gain_loaded)
            pool.wait_ge(normed_ready, NORMED["pre_mlp0"] + all_normed)
            load_gain(gain_pre[:, :], kv_g, pre_gain_loaded)
            zero_branch("turn_mlp0")
            scale_by_gain("post_mlp0")
            inverse_rms("post_mlp0", D)
            inverse_rms("pre_kv", D, range(TB))
            load_gain(gain_post[:, :], b_post_g[0], post_gain_loaded)
            pool.wait_ge(normed_ready, NORMED["pre_kv"] + all_normed)
            load_gain(gain_pre[:, :], b_pre_g[0], pre_gain_loaded)
            pool.wait_ge(normed_ready, NORMED["pre_q"] + all_normed)
            load_gain(gain_pre[:, :], mlp_pre_g[1], pre_gain_loaded)
            for t in range(HEADS):
                pool.wait_ge(stick_exp, t + 1)
                diag = probs[:, t % 2, :].rearrange("p (b n) -> p b n", b=3)[:, 0:3:2, :]
                nc.gpsimd.tensor_tensor(diag, diag, strict2, ALU.mult).then_inc(stick_ready, 1)
            scale_by_gain("post_stick")
            inverse_rms("post_stick", D)
            inverse_rms("pre_mlp1", D, range(TB))
            load_gain(gain_post[:, :], mlp_post_g[1], post_gain_loaded)
            zero_branch("turn_mlp1")
            scale_by_gain("post_mlp1")
            inverse_rms("post_mlp1", D)

        @block.scalar
        def _(act):
            def split_hi(p, part=0):
                if p % 2 == 0:
                    c = p // 2
                    act.wait_ge(raw_loaded[c % RAW_SLOTS],
                                16 * (c // RAW_SLOTS + 1) + part * (16 * MLP_CHUNKS // RAW_SLOTS))
                moves = split_moves(p)
                for src, hi, lo in moves[:-1]:
                    nc.scalar.activation(hi, src, ACT.Copy)
                src, hi, lo = moves[-1]
                nc.scalar.activation(hi, src, ACT.Copy).then_inc(hi_ready, 1)

            def split_ahead(p, part=0):
                if p + PIECE_SLOTS < PIECES:
                    signal, value = USED[p]
                    if signal == "bank_full":
                        act.wait_ge(bank_full, value + part * MLP_BANKS)
                    else:
                        act.wait_ge(piece_used, value + part * MLP_USED)
                    split_hi(p + PIECE_SLOTS, part)

            def sum_squares(n, col, src):
                if n:
                    act.wait_ge(squares_ready, n)
                nc.scalar.activation(junk[:, 0:src.shape[-1]], src, ACT.Square,
                                     accum_out=col).then_inc(squares_ready, 1)

            def branch_squares(name, g):
                for b in range(TB):
                    act.wait_ge(bank_free, BRANCH_BANK[name] + TB * g + b + 1)
                    sum_squares(SQUARES[name, None] + TB * g + b,
                                squares[:, STAT[name, None] + b, g:g + 1],
                                branch[:, b, g * NCOL:(g + 1) * NCOL])

            def resid_squares(name, waits):
                for b in range(TB):
                    for h in range(2):
                        waits(b, h)
                        sum_squares(SQUARES[name, b] + h, squares[:, STAT[name, b], h:h + 1],
                                    resid[:, b, h * D // 2:(h + 1) * D // 2])

            def turn_hi(name, k0, dst=xT, last_piece=None):
                for i in range(BANK_END[name] - BANK0[name]):
                    if i == 4 and last_piece is not None:
                        split_ahead(last_piece)
                    s = BANK0[name] + i
                    act.wait_ge(bank_full, s + 1)
                    nc.scalar.activation(dst[:, k0 + 2 * i:k0 + 2 * i + 2, 0, :],
                                         bank_of(s).rearrange("p (k t) -> p k t", k=2),
                                         ACT.Copy).then_inc(turned_hi, 1)

            def take_half(s, off, i, scale=1.0, before=None):
                if before is not None:
                    act.wait_ge(bank_free, before + 1)
                act.wait_ge(bank_full, s + 1 + off)
                nc.scalar.activation(half_sum[:, i % 4, :], bank_of(s)[:, SEQ:2 * SEQ], ACT.Copy,
                                     scale=scale).then_inc(half_ready, 1)

            def swap_rope(s, n):
                act.wait_ge(bank_free, s + 1)
                for q in (2, 3):
                    src = full_sum[32 * (q ^ 1):32 * (q ^ 1) + 32, 2 * (n % 2), :]
                    nc.scalar.activation(full_sum[32 * q:32 * q + 32, 2 * (n % 2) + 1, :], src,
                                         ACT.Copy).then_inc(swapped_high, 1)

            def feature_stage(name, scale):
                for i in range(UNIT_PIECES):
                    if i % GROUP_PIECES == GROUP_PIECES - 1:
                        for f in range(4):
                            s = BANK0[name] + i // GROUP_PIECES * 4 + f
                            take_half(s, 0, f, scale, before=s - 4 if i >= GROUP_PIECES else None)
                    split_ahead(2 * CHUNK0[name] + i)

            def token_stage(name, norm=None, p0=None, part=0, last=False, first=0):
                p0 = 2 * CHUNK0[name] if p0 is None else p0
                for i in range(first, UNIT_PIECES):
                    if i < UNIT_PIECES - (PIECE_SLOTS if last else 1 if norm else 0):
                        split_ahead(p0 + i, part)
                    if norm and i >= GROUP_PIECES and i % GROUP_PIECES == 1:
                        branch_squares(norm, i // GROUP_PIECES - 1)
                if norm:
                    branch_squares(norm, QUARTERS - 1)

            def fill_ahead(name, step):
                k = (step - FILL_LAG - 2) // 2
                if step % 2 == 0 and k >= 0:
                    split_ahead(2 * CHUNK0[name] + k)

            def updated(post):
                return lambda b, h: act.wait_ge(resid_ready, RESIDUAL[post] + 2 * b + h + 1)

            resid_squares("pre_mla", lambda b, h: act.wait_ge(x_loaded[b], 16))
            for p in range(PIECE_SLOTS):
                split_hi(p)
            turn_hi("turn_mla", 0)
            for i in range(2 * (CHUNK0["k_rope"] - CHUNK0["latents"])):
                split_ahead(2 * CHUNK0["latents"] + i)
            for b in range(TB):
                for part in range(2):
                    act.wait_ge(bank_free, BANK0["latents"] + TB * part + b + 1)
                    i = 2 * b + part
                    sum_squares(SQUARES["latents", None] + i, squares[:, STAT["latents", None] + i, 0:1],
                                branch[:, b, part * LORA:(part + 1) * LORA])
            take_half(BANK0["k_rope"], 0, 0)
            swap_rope(BANK0["k_rope"], 0)
            for i in range(2):
                split_ahead(2 * CHUNK0["k_rope"] + i)
            turn_hi("turn_latents", KT - 2 * LT)
            for i in range(HEADS // 2):
                s = BANK0["q_mla"] + 3 * i
                split_ahead(2 * (CHUNK0["q_mla"] + i))
                for f in range(3):
                    take_half(s + f, 0, f, MLA_SCALE, before=s + f - 3 if i else None)
                split_ahead(2 * (CHUNK0["q_mla"] + i) + 1)
                swap_rope(s + 2, 1 + i)
            for i in range(HEADS // 2):
                s = BANK0["kv_mla"] + 4 * i
                split_ahead(2 * (CHUNK0["kv_mla"] + i))
                for f in range(2):
                    take_half(s + f, 0, f, before=s + f - 4 if i else None)
                split_ahead(2 * (CHUNK0["kv_mla"] + i) + 1)

            def out_split(t, s):
                act.wait_ge(bank_full, s + 1)
                nc.scalar.activation(xT[:, t, 0, :], bank_of(s)[:, 0:SEQ], ACT.Copy).then_inc(out_hi, 1)

            for step in range(HEADS + 2):
                if 1 <= step <= HEADS:
                    t = step - 1
                    act.wait_ge(sum_inverse, t + 1)
                    for q, (c0, c1) in enumerate(((0, P), (P, 3 * P))):
                        i = 2 * t + q
                        nc.scalar.activation(probs[:, t % 2, c0:c1], probs[:, t % 2, c0:c1], ACT.Copy,
                                             scale=rows[:, 2, i:i + 1]).then_inc(probs_ready, 1)
                if step < HEADS:
                    t = step
                    act.wait_ge(row_max, 2 * t + 2)
                    for q, (c0, c1) in enumerate(((0, P), (P, 3 * P))):
                        i = 2 * t + q
                        nc.scalar.activation(probs[:, t % 2, c0:c1], probs[:, t % 2, c0:c1], ACT.Exp,
                                             bias=rows[:, 0, i:i + 1],
                                             accum_out=rows[:, 1, i:i + 1]).then_inc(exp_ready, 1)
                if step >= 2:
                    out_split(step - 2, MLA_BANK["out", step - 2])
                fill_ahead("mla_out", step)
            token_stage("mla_out", "post_mla", first=FILLED - 1)
            resid_squares("pre_mlp0", updated("post_mla"))
            turn_hi("turn_mlp0", 0, last_piece=2 * CHUNK0["mlp0"] - 1)

            def mlp_part(name, part, norm=None, last=False):
                p0, s0 = 2 * CHUNK0[name], BANK0[name]
                soff, foff = part * MLP_BANKS, part * FEATURE_BANKS
                for i in range(UNIT_PIECES):
                    if i % GROUP_PIECES == GROUP_PIECES - 1:
                        g = i // GROUP_PIECES
                        for f in range(5):
                            if f < 4:
                                take_half(s0 + 4 * g + f, soff, f)
                            if f >= 1:
                                k = 4 * g + f - 1
                                act.wait_ge(relu2_ready, HIDDEN[name] + k + 1 + foff)
                                nc.scalar.activation(hidT[:, k, 0, :], full_sum[:, k % 4, :],
                                                     ACT.Copy).then_inc(hidden_hi, 1)
                    split_ahead(p0 + i, part)
                token_stage(name, norm, p0 + UNIT_PIECES, part, last)

            with act.Fori(0, FFN_PARTS - 1) as part:
                mlp_part("mlp0", part)
            mlp_part("mlp0", FFN_PARTS - 1, "post_mlp0")
            resid_squares("pre_kv", updated("post_mlp0"))
            turn_hi("turn_kv", 0, last_piece=2 * CHUNK0["k_shared"] - 1)

            feature_stage("k_shared", 1.0)
            token_stage("v_shared")
            turn_hi("turn_q", 0)
            feature_stage("q_stick", STICK_SCALE)
            nc.scalar.preload_act_table_set("natural_log_exp_and_others")
            for step in range(HEADS + 2):
                if step < HEADS:
                    t = step
                    s = STICK_BANK["logits", t]
                    tail = soft[:, t % 2, :]
                    act.wait_ge(logit_ready, t + 1)
                    nc.scalar.activation(tail, bank_of(s)[:, 0:384], ACT.Abs).then_inc(abs_ready, 1)
                    act.wait_ge(abs_ready, t + 1)
                    nc.scalar.activation(tail, tail, ACT.Exp, scale=-1.0).then_inc(exp_abs, 1)
                    act.wait_ge(exp_abs, t + 1)
                    nc.scalar.activation(tail, tail, ACT.Ln, bias=1.0).then_inc(log_term, 1)
                if 1 <= step <= HEADS:
                    t = step - 1
                    act.wait_ge(bank_free, STICK_BANK["logits", t] + 1)
                    nc.scalar.activation(probs[:, t % 2, :], probs[:, t % 2, :], ACT.Exp).then_inc(stick_exp, 1)
                if step >= 2:
                    out_split(step - 2, STICK_BANK["out", step - 2])
                fill_ahead("stick_out", step)
            token_stage("stick_out", "post_stick", first=FILLED - 1)
            resid_squares("pre_mlp1", updated("post_stick"))
            turn_hi("turn_mlp1", 0, last_piece=2 * CHUNK0["mlp1"] - 1)
            with act.Fori(0, FFN_PARTS - 1) as part:
                mlp_part("mlp1", part)
            mlp_part("mlp1", FFN_PARTS - 1, "post_mlp1", last=True)

        @block.tensor
        def _(pe):
            def open_bank(s, off=0):
                if BEFORE[s] is not None:
                    pe.wait_ge(bank_free, BEFORE[s] + 1 + off)

            def piece(p, off=0, k=2):
                pe.wait_ge(lo_ready, p + 1 + off)
                n = 2 * (NOPE + ROPE) if CHUNK0["q_mla"] <= p // 2 < CHUNK0["kv_mla"] else PIECE // k
                return [w[:, p % PIECE_SLOTS, 0:k * n].rearrange("p (k n) -> p k n", k=k) for w in (whi, wlo)]

            def feature_block(s, hi, lo, op, first, last):
                nc.tensor.matmul(bank_of(s), hi, op, start=first, stop=False)
                return nc.tensor.matmul(bank_of(s)[:, 0:SEQ], lo, op[:, 0, :], start=False, stop=last)

            def token_block(dst, hi, lo, op, b, first, last):
                t = slice(b * P, (b + 1) * P)
                nc.tensor.matmul(dst, op[:, 0, t], hi, start=first, stop=False)
                nc.tensor.matmul(dst, op[:, 0, t], lo, start=False, stop=False)
                return nc.tensor.matmul(dst, op[:, 1, t], hi, start=False, stop=last)

            def feature_unit(p0, s0, poff=0, soff=0, op=xT, ready=None):
                for i in range(UNIT_PIECES):
                    g, kp = divmod(i, GROUP_PIECES)
                    if ready and g == 0:
                        ready(kp)
                    hi, lo = piece(p0 + i, poff)
                    for f in range(4):
                        s = s0 + 4 * g + f
                        if kp == 0:
                            open_bank(s, soff)
                        for k in range(2):
                            kt = 2 * kp + k
                            mm = feature_block(s, hi[:, k, f * P:(f + 1) * P], lo[:, k, f * P:(f + 1) * P],
                                               op[:, kt, :, :], kt == 0, kt == KT - 1)
                        if kp == GROUP_PIECES - 1:
                            mm.then_inc(bank_full, 1)
                    if kp < GROUP_PIECES - 1:
                        mm.then_inc(piece_used, 1)

            def token_piece(p, s, kp, b, poff=0, soff=0, op=xT):
                hi, lo = piece(p, poff)
                if kp == 0:
                    open_bank(s, soff)
                for k in range(2):
                    kt = 2 * kp + k
                    mm = token_block(bank_of(s), hi[:, k, :], lo[:, k, :], op[:, kt, :, :], b,
                                     kt == 0, kt == KT - 1)
                if kp == GROUP_PIECES - 1:
                    mm.then_inc(bank_full, 1)
                elif b == TB - 1:
                    mm.then_inc(piece_used, 1)

            def token_unit(p0, s0, poff=0, soff=0, op=xT, groups=D // NCOL, ready=None, first=0):
                for i in range(first, groups * GROUP_PIECES):
                    g, kp = divmod(i, GROUP_PIECES)
                    if ready and g == 0:
                        ready(kp)
                    for b in range(TB):
                        token_piece(p0 + i, s0 + TB * g + b, kp, b, poff, soff, op)

            def fill(name, banks, step):
                k, b = divmod(step - FILL_LAG, 2)
                if k >= 0:
                    pe.wait_ge(bank_free, banks["out", 2 * k + 1] + 1)
                    token_piece(2 * CHUNK0[name] + k, BANK0[name] + b, k, b)

            def turn(name, tiles, normed=None):
                for i in range(tiles // 2):
                    if normed and i % 2 == 0:
                        pe.wait_ge(normed_ready, NORMED[normed] + TB * (i // 2 + 1))
                    s = BANK0[name] + i
                    open_bank(s)
                    for j in range(4):
                        kt, b = 2 * i + j // 2, j % 2
                        mm = nc.tensor.transpose(bank_of(s)[:, j * P:(j + 1) * P],
                                                 branch[:, b, kt * P:(kt + 1) * P], ident)
                    mm.then_inc(bank_full, 1)

            def turned(name):
                return lambda kp: pe.wait_ge(bank_free, BANK0[name] + kp + 1)

            pe.wait_ge(con_loaded, 16)
            turn("turn_mla", KT, "pre_mla")
            token_unit(2 * CHUNK0["latents"], BANK0["latents"], groups=2, ready=turned("turn_mla"))
            s = BANK0["k_rope"]
            open_bank(s)
            for i in range(2):
                hi, lo = piece(2 * CHUNK0["k_rope"] + i, k=KT // 2)
                for k in range(KT // 2):
                    kt = i * KT // 2 + k
                    mm = feature_block(s, hi[:, k, :], lo[:, k, :], xT[:, kt, :, :], kt == 0, kt == KT - 1)
                mm.then_inc(piece_used if i == 0 else bank_full, 1)
            pe.wait_ge(latent_normed, 2 * TB)
            turn("turn_latents", 2 * LT)
            cq, ckv = KT - 2 * LT, KT - LT
            for i in range(HEADS // 2):
                s = BANK0["q_mla"] + 3 * i
                for j in range(2):
                    if i == 0:
                        pe.wait_ge(bank_free, BANK0["turn_latents"] + j + 1)
                    hi, lo = piece(2 * (CHUNK0["q_mla"] + i) + j)
                    for f in range(3):
                        if j == 0:
                            open_bank(s + f)
                        for k in range(2):
                            kt = 2 * j + k
                            cols = slice(f * P, (f + 1) * P)
                            mm = feature_block(s + f, hi[:, k, cols], lo[:, k, cols], xT[:, cq + kt, :, :], kt == 0, kt == LT - 1)
                        if j == 1:
                            mm.then_inc(bank_full, 1)
                    if j == 0:
                        mm.then_inc(piece_used, 1)
            for i in range(HEADS // 2):
                s = BANK0["kv_mla"] + 4 * i
                for j in range(2):
                    if i == 0:
                        pe.wait_ge(bank_free, BANK0["turn_latents"] + 2 + j + 1)
                    hi, lo = piece(2 * (CHUNK0["kv_mla"] + i) + j)
                    for f in range(2):
                        if j == 0:
                            open_bank(s + f)
                        for k in range(2):
                            kt = 2 * j + k
                            cols = slice(2 * f * P, (2 * f + 1) * P)
                            mm = feature_block(s + f, hi[:, k, cols], lo[:, k, cols], xT[:, ckv + kt, :, :],
                                               kt == 0, kt == LT - 1)
                        if j == 1:
                            mm.then_inc(bank_full, 1)
                    for b in range(TB):
                        if j == 0:
                            open_bank(s + 2 + b)
                        dst = bank_of(s + 2 + b)[:, 0:2 * P]
                        for k in range(2):
                            kt = 2 * j + k
                            h, l = (w[:, k, :].rearrange("p (h n) -> p h n", n=P)[:, 1:4:2, :] for w in (hi, lo))
                            mm = token_block(dst, h, l, xT[:, ckv + kt, :, :], b, kt == 0, kt == LT - 1)
                        if j == 1:
                            mm.then_inc(bank_full, 1)
                    if j == 0:
                        mm.then_inc(piece_used, 1)

            def weighted_values(t, s, w):
                h = slice(t * P, (t + 1) * P)
                open_bank(s)
                nc.tensor.matmul(bank_of(s)[:, 0:SEQ], val[:, 0, h], w[:, 0:SEQ], start=True, stop=False)
                nc.tensor.matmul(bank_of(s)[:, P:SEQ], val[:, 1, h], w[:, SEQ:3 * P], start=False,
                                 stop=True).then_inc(bank_full, 1)

            pe.wait_ge(bank_free, BANK_END["kv_mla"])
            pe.wait_ge(rope_ready, 1 + HEADS // 2)
            for step in range(HEADS + 2):
                if step < HEADS:
                    t = step
                    s = MLA_BANK["scores", t]
                    open_bank(s)
                    r = slice(ROPE * (t % 2), ROPE * (t % 2) + ROPE)
                    for q, (c0, keys) in enumerate(((0, P), (P, 2 * P))):
                        qs = slice(q * P, (q + 1) * P)
                        dst = bank_of(s)[:, c0:c0 + keys]
                        nc.tensor.matmul(dst, queryT[:, t, qs], keyT[:, t, 0:keys], start=True, stop=False)
                        mm = nc.tensor.matmul(dst, qropeT[r, t // 2, qs], kropeT[r, 0:keys], start=False, stop=True)
                    mm.then_inc(bank_full, 1)
                if step >= 2:
                    t = step - 2
                    pe.wait_ge(bank_free, MLA_BANK["turned", t] + 1)
                    weighted_values(t, MLA_BANK["out", t], probsT[:, t % 2, :])
                fill("mla_out", MLA_BANK, step)
                if 1 <= step <= HEADS:
                    t = step - 1
                    s = MLA_BANK["turned", t]
                    open_bank(s)
                    pe.wait_ge(probs_ready, 2 * t + 2)
                    for j in range(3):
                        mm = nc.tensor.transpose(bank_of(s)[:, j * P:(j + 1) * P],
                                                 probs[:, t % 2, j * P:(j + 1) * P], ident)
                    mm.then_inc(bank_full, 1)
            pe.wait_ge(bank_free, BANK_END["mla"])
            token_unit(2 * CHUNK0["mla_out"], BANK0["mla_out"], first=FILLED)

            def mlp(name, turn_name, loop_parts):
                turn("turn_" + name, KT, turn_name)

                def one(part):
                    poff, soff, foff = part * MLP_PIECES, part * MLP_BANKS, part * FEATURE_BANKS
                    feature_unit(2 * CHUNK0[name], BANK0[name], poff, soff, ready=turned("turn_" + name))

                    def hidden(kp):
                        pe.wait_ge(hidden_ready, HIDDEN[name] + 2 * kp + 2 + foff)

                    token_unit(2 * CHUNK0[name] + UNIT_PIECES, BANK0[name] + FEATURE_BANKS, poff, soff,
                               op=hidT, ready=hidden)

                with pe.Fori(0, FFN_PARTS) as part:
                    one(part)

            mlp("mlp0", "pre_mlp0", FFN_PARTS)
            turn("turn_kv", KT, "pre_kv")
            feature_unit(2 * CHUNK0["k_shared"], BANK0["k_shared"], ready=turned("turn_kv"))
            token_unit(2 * CHUNK0["v_shared"], BANK0["v_shared"])
            turn("turn_q", KT, "pre_q")
            feature_unit(2 * CHUNK0["q_stick"], BANK0["q_stick"], ready=turned("turn_q"))

            pe.wait_ge(bank_free, BANK_END["q_stick"])
            suffix, later = con[:, SUFFIX:SUFFIX + P], con[:, LATER:LATER + P]
            for step in range(HEADS + 2):
                if step < HEADS:
                    t = step
                    s = STICK_BANK["logits", t]
                    open_bank(s)
                    z = bank_of(s)
                    nc.tensor.matmul(z[:, 0:SEQ], keyT[:, t, 0:P], queryT[:, t, :], start=True, stop=False,
                                     skip_group_check=True)
                    nc.tensor.matmul(z[:, SEQ:3 * P], keyT[:, t, P:SEQ], queryT[:, t, P:SEQ], start=False,
                                     stop=False, skip_group_check=True).then_inc(logit_ready, 1)
                fill("stick_out", STICK_BANK, step)
                if 1 <= step <= HEADS:
                    t = step - 1
                    z, sp_ = bank_of(STICK_BANK["logits", t]), soft[:, 2 + t % 2, :]
                    pe.wait_ge(masked_softplus, t + 1)
                    nc.tensor.matmul(z[:, 0:SEQ], suffix, sp_[:, 0:SEQ], start=False, stop=False,
                                     skip_group_check=True)
                    nc.tensor.matmul(z[:, P:SEQ], later, sp_[:, SEQ:3 * P], start=False, stop=False,
                                     skip_group_check=True)
                    nc.tensor.matmul(z[:, SEQ:3 * P], suffix, sp_[:, SEQ:3 * P], start=False, stop=True,
                                     skip_group_check=True).then_inc(bank_full, 1)
                if step >= 2:
                    t = step - 2
                    pe.wait_ge(stick_ready, t + 1)
                    weighted_values(t, STICK_BANK["out", t], probs[:, t % 2, :])
            pe.wait_ge(bank_free, BANK_END["stick"])
            token_unit(2 * CHUNK0["stick_out"], BANK0["stick_out"], first=FILLED)
            mlp("mlp1", "pre_mlp1", FFN_PARTS)

        @block.vector
        def _(dve):
            def split_lo(p, part=0):
                dve.wait_ge(hi_ready, p + 1 + part * MLP_PIECES)
                moves = split_moves(p)
                for src, hi, lo in moves[:-1]:
                    nc.vector.tensor_tensor(lo, src, hi.bitcast(F32), ALU.subtract)
                src, hi, lo = moves[-1]
                nc.vector.tensor_tensor(lo, src, hi.bitcast(F32), ALU.subtract).then_inc(lo_ready, 1)

            def split_ahead(p, part=0):
                if p + PIECE_SLOTS < PIECES:
                    split_lo(p + PIECE_SLOTS, part)

            def add_halves(dst, s, off, i, half, scale=1.0):
                dve.wait_ge(half_ready, half + 1)
                nc.vector.scalar_tensor_tensor(out=dst, in0=bank_of(s)[:, 0:SEQ], scalar=scale,
                                               in1=half_sum[:, i % 4, :], op0=ALU.mult,
                                               op1=ALU.add).then_inc(bank_free, 1)

            def swap_rope(s, n):
                dve.wait_ge(bank_free, s + 1)
                for q in (0, 1):
                    src = full_sum[32 * (q ^ 1):32 * (q ^ 1) + 32, 2 * (n % 2), :]
                    nc.vector.tensor_copy(full_sum[32 * q:32 * q + 32, 2 * (n % 2) + 1, :],
                                          src).then_inc(swapped_low, 1)

            def norm_rows(name, stat_of, q):
                cols = slice(q * NCOL, (q + 1) * NCOL)
                dve.wait_ge(pre_gain_loaded, 16 * PRE_GAIN_LOADS[name])
                for b in range(TB):
                    i = STAT[stat_of, b]
                    dve.wait_ge(rms_ready, REQUEST[stat_of, b] + 1)
                    nc.vector.scalar_tensor_tensor(out=branch[:, b, cols], in0=resid[:, b, cols],
                                                   scalar=stat[:, 2, i:i + 1], in1=gain_pre[:, cols],
                                                   op0=ALU.mult, op1=ALU.mult).then_inc(normed_ready, 1)

            def sum_parts(name, b=None):
                r, i = REQUEST[name, b], STAT[name, b]
                _, _, cols, parts = NORMS[r]
                dve.wait_ge(squares_ready, SQUARES[name, b] + cols * parts)
                nc.vector.tensor_reduce(stat[:, 0, i:i + cols], squares[:, i:i + cols, 0:parts], AX_X,
                                        ALU.add).then_inc(sum_ready, 1)

            def add_branch(name, pre=None):
                g = QUARTERS - 1
                n = list(RESIDUAL).index(name)
                dve.wait_ge(post_gain_loaded, 16 * POST_GAIN_LOADS[name])
                for b in range(TB):
                    last = branch[:, b, g * NCOL:(g + 1) * NCOL]
                    dve.wait_ge(squares_ready, SQUARES[name, None] + TB * g + b + 1)
                    if b == TB - 1:
                        sum_parts(name)
                    nc.vector.tensor_tensor(last, last, gain_post[:, g * NCOL:(g + 1) * NCOL],
                                            ALU.mult).then_inc(last_scaled, 1)
                dve.wait_ge(gain_scaled, GAINED[name] + g * TB)
                dve.wait_ge(rms_ready, REQUEST[name, None] + 1)
                dve.wait_ge(last_scaled, TB * (n + 1))
                for b in range(TB):
                    i = STAT[name, None] + b
                    for h in range(2):
                        cols = slice(h * D // 2, (h + 1) * D // 2)
                        nc.vector.scalar_tensor_tensor(out=resid[:, b, cols], in0=branch[:, b, cols],
                                                       scalar=stat[:, 2, i:i + 1], in1=resid[:, b, cols],
                                                       op0=ALU.mult, op1=ALU.add).then_inc(resid_ready, 1)
                        if pre and b and h:
                            sum_parts(pre, b - 1)
                if pre:
                    sum_parts(pre, TB - 1)

            def norm_and_turn(turn_name, name, last_piece=None):
                norm_rows(name, name, 0)
                for q in range(QUARTERS):
                    if q + 1 < QUARTERS:
                        norm_rows(name, name, q + 1)
                    if q == 2 and last_piece is not None:
                        split_ahead(last_piece)
                    turn_lo(turn_name, 0, range(2 * q, 2 * q + 2))

            def turn_lo(name, k0, banks):
                for i in banks:
                    s = BANK0[name] + i
                    dve.wait_ge(turned_hi, TURN[name] + i + 1)
                    k = slice(k0 + 2 * i, k0 + 2 * i + 2)
                    nc.vector.tensor_tensor(xT[:, k, 1, :], bank_of(s).rearrange("p (k t) -> p k t", k=2),
                                            xT[:, k, 0, :].bitcast(F32), ALU.subtract).then_inc(bank_free, 1)

            def feature_stage(name, dst, scale=1.0):
                for i in range(UNIT_PIECES):
                    if i % GROUP_PIECES == GROUP_PIECES - 1:
                        for f in range(4):
                            k = i // GROUP_PIECES * 4 + f
                            add_halves(dst[:, k, :], BANK0[name] + k, 0, f, HALF[name] + k, scale)
                    split_ahead(2 * CHUNK0[name] + i)

            def fill_ahead(name, step):
                k = (step - FILL_LAG - 2) // 2
                if step % 2 == 0 and k >= 0:
                    split_ahead(2 * CHUNK0[name] + k)

            def token_stage(name, dst, groups=D // NCOL, norm=False, first=0):
                for i in range(first, groups * GROUP_PIECES):
                    if i % GROUP_PIECES == GROUP_PIECES - 1:
                        g = i // GROUP_PIECES
                        for b in range(TB):
                            s = BANK0[name] + TB * g + b
                            dve.wait_ge(bank_full, s + 1)
                            nc.vector.tensor_copy(dst[:, b, g * NCOL:(g + 1) * NCOL],
                                                  bank_of(s)).then_inc(bank_free, 1)
                    if not norm or i < UNIT_PIECES - 1:
                        split_ahead(2 * CHUNK0[name] + i)

            for b in range(TB):
                sum_parts("pre_mla", b)
            for p in range(PIECE_SLOTS):
                split_lo(p)
            norm_and_turn("turn_mla", "pre_mla")
            token_stage("latents", branch, groups=2)
            add_halves(full_sum[:, 0, :], BANK0["k_rope"], 0, 0, HALF["k_rope"])
            swap_rope(BANK0["k_rope"], 0)
            sum_parts("latents")
            dve.wait_ge(pre_gain_loaded, 16 * PRE_GAIN_LOADS["latents"])
            dve.wait_ge(rms_ready, REQUEST["latents", None] + 1)
            for b in range(TB):
                for part in range(2):
                    i = STAT["latents", None] + 2 * b + part
                    c = branch[:, b, part * LORA:(part + 1) * LORA]
                    nc.vector.scalar_tensor_tensor(out=c, in0=c, scalar=stat[:, 2, i:i + 1],
                                                   in1=gain_pre[:, part * LORA:(part + 1) * LORA],
                                                   op0=ALU.mult, op1=ALU.mult).then_inc(latent_normed, 1)
            for i in range(2):
                split_ahead(2 * CHUNK0["k_rope"] + i)
            turn_lo("turn_latents", KT - 2 * LT, range(LT))
            for i in range(HEADS // 2):
                s, h = BANK0["q_mla"] + 3 * i, HALF["q_mla"] + 3 * i
                split_ahead(2 * (CHUNK0["q_mla"] + i))
                for f in range(2):
                    add_halves(queryT[:, 2 * i + f, :], s + f, 0, f, h + f, MLA_SCALE)
                n = 1 + i
                if n >= 2:
                    dve.wait_ge(rope_ready, n - 1)
                add_halves(full_sum[:, 2 * (n % 2), :], s + 2, 0, 2, h + 2, MLA_SCALE)
                split_ahead(2 * (CHUNK0["q_mla"] + i) + 1)
                swap_rope(s + 2, n)
            for i in range(HEADS // 2):
                s, h = BANK0["kv_mla"] + 4 * i, HALF["kv_mla"] + 2 * i
                split_ahead(2 * (CHUNK0["kv_mla"] + i))
                for f in range(2):
                    add_halves(keyT[:, 2 * i + f, :], s + f, 0, f, h + f)
                for b in range(TB):
                    dve.wait_ge(bank_full, s + 3 + b)
                    nc.vector.tensor_copy(val[:, b, 2 * i * P:2 * (i + 1) * P],
                                          bank_of(s + 2 + b)[:, 0:2 * P]).then_inc(bank_free, 1)
                split_ahead(2 * (CHUNK0["kv_mla"] + i) + 1)

            def out_rest(t, s, n):
                dve.wait_ge(out_hi, n + 1)
                nc.vector.tensor_tensor(xT[:, t, 1, :], bank_of(s)[:, 0:SEQ], xT[:, t, 0, :].bitcast(F32),
                                        ALU.subtract).then_inc(bank_free, 1)

            for step in range(HEADS + 2):
                if 1 <= step <= HEADS:
                    t = step - 1
                    dve.wait_ge(exp_ready, 2 * t + 2)
                    nc.vector.reciprocal(rows[:, 2, 2 * t:2 * t + 2],
                                         rows[:, 1, 2 * t:2 * t + 2]).then_inc(sum_inverse, 1)
                if step < HEADS:
                    t = step
                    s = MLA_BANK["scores", t]
                    pr = probs[:, t % 2, :]
                    dve.wait_ge(bank_full, s + 1)
                    nc.vector.tensor_tensor(pr, bank_of(s)[:, 0:3 * P], con[:, CAUSAL:CAUSAL + 3 * P],
                                            ALU.add).then_inc(bank_free, 1)
                    dve.wait_ge(bank_free, s + 1)
                    for q, (c0, c1) in enumerate(((0, P), (P, 3 * P))):
                        nc.vector.tensor_reduce(rows[:, 0, 2 * t + q:2 * t + q + 1], pr[:, c0:c1], AX_X,
                                                ALU.max, negate=True).then_inc(row_max, 1)
                if step >= 2:
                    out_rest(step - 2, MLA_BANK["out", step - 2], step - 2)
                if 1 <= step <= HEADS:
                    t = step - 1
                    s = MLA_BANK["turned", t]
                    dve.wait_ge(bank_full, s + 1)
                    nc.vector.tensor_copy(probsT[:, t % 2, :], bank_of(s)[:, 0:3 * P]).then_inc(bank_free, 1)
                fill_ahead("mla_out", step)
            token_stage("mla_out", branch, norm=True, first=FILLED - 1)
            add_branch("post_mla", "pre_mlp0")
            norm_and_turn("turn_mlp0", "pre_mlp0", 2 * CHUNK0["mlp0"] - 1)

            def mlp_part(name, part, norm=None, last=False):
                p0, s0 = 2 * CHUNK0[name], BANK0[name]
                soff, foff = part * MLP_BANKS, part * FEATURE_BANKS
                for i in range(UNIT_PIECES):
                    if i % GROUP_PIECES == GROUP_PIECES - 1:
                        g = i // GROUP_PIECES
                        for f in range(5):
                            if f < 4:
                                k = 4 * g + f
                                v = full_sum[:, f, :]
                                if k >= 4:
                                    dve.wait_ge(hidden_ready, HIDDEN[name] + k - 3 + foff)
                                add_halves(v, s0 + k, soff, f, HALF[name] + k + foff)
                                dve.wait_ge(bank_free, s0 + k + 1 + soff)
                                nc.vector.scalar_tensor_tensor(out=v, in0=v, scalar=0.0, in1=v, op0=ALU.max,
                                                               op1=ALU.mult).then_inc(relu2_ready, 1)
                            if f >= 1:
                                k = 4 * g + f - 1
                                dve.wait_ge(hidden_hi, HIDDEN[name] + k + 1 + foff)
                                nc.vector.tensor_tensor(hidT[:, k, 1, :], full_sum[:, f - 1, :],
                                                        hidT[:, k, 0, :].bitcast(F32),
                                                        ALU.subtract).then_inc(hidden_ready, 1)
                    split_ahead(p0 + i, part)
                for i in range(UNIT_PIECES):
                    if i % GROUP_PIECES == GROUP_PIECES - 1:
                        g = i // GROUP_PIECES
                        for b in range(TB):
                            s = s0 + FEATURE_BANKS + TB * g + b
                            dst = branch[:, b, g * NCOL:(g + 1) * NCOL]
                            dve.wait_ge(bank_full, s + 1 + soff)
                            nc.vector.tensor_tensor(dst, bank_of(s), dst, ALU.add).then_inc(bank_free, 1)
                    if i < UNIT_PIECES - (PIECE_SLOTS if last else 1 if norm else 0):
                        split_ahead(p0 + UNIT_PIECES + i, part)

            dve.wait_ge(branch_zeroed, ZEROED["mlp0"])
            with dve.Fori(0, FFN_PARTS - 1) as part:
                mlp_part("mlp0", part)
            mlp_part("mlp0", FFN_PARTS - 1, "post_mlp0")
            add_branch("post_mlp0", "pre_kv")
            norm_and_turn("turn_kv", "pre_kv", 2 * CHUNK0["k_shared"] - 1)
            feature_stage("k_shared", keyT)
            for q in range(QUARTERS):
                norm_rows("pre_q", "pre_kv", q)
            token_stage("v_shared", val)
            turn_lo("turn_q", 0, range(TURN_BANKS))
            feature_stage("q_stick", queryT, STICK_SCALE)

            for step in range(HEADS + 2):
                if 1 <= step <= HEADS:
                    t = step - 1
                    s = STICK_BANK["logits", t]
                    dve.wait_ge(bank_full, s + 1)
                    nc.vector.tensor_scalar(probs[:, t % 2, :], bank_of(s)[:, 0:3 * P], 0.0, None,
                                            ALU.min).then_inc(bank_free, 1)
                if step < HEADS:
                    t = step
                    s = STICK_BANK["logits", t]
                    spt = soft[:, 2 + t % 2, :]
                    dve.wait_ge(log_term, t + 1)
                    nc.vector.scalar_tensor_tensor(out=spt, in0=bank_of(s)[:, 0:3 * P], scalar=0.0,
                                                   in1=soft[:, t % 2, :], op0=ALU.max,
                                                   op1=ALU.add).then_inc(softplus, 1)
                    diag = spt.rearrange("p (b n) -> p b n", b=3)[:, 0:3:2, :]
                    dve.wait_ge(softplus, t + 1)
                    nc.vector.tensor_tensor(diag, diag, strict2, ALU.mult).then_inc(masked_softplus, 1)
                if step >= 2:
                    out_rest(step - 2, STICK_BANK["out", step - 2], HEADS + step - 2)
                fill_ahead("stick_out", step)
            token_stage("stick_out", branch, norm=True, first=FILLED - 1)
            add_branch("post_stick", "pre_mlp1")
            norm_and_turn("turn_mlp1", "pre_mlp1", 2 * CHUNK0["mlp1"] - 1)
            dve.wait_ge(branch_zeroed, ZEROED["mlp1"])
            with dve.Fori(0, FFN_PARTS - 1) as part:
                mlp_part("mlp1", part)
            mlp_part("mlp1", FFN_PARTS - 1, "post_mlp1", last=True)
            add_branch("post_mlp1")


_INS = ["x", "a_pre_g", "a_post_g", "a_w_dq_dkv", "a_q_norm_g", "a_kv_norm_g", "a_w_uq", "a_w_ukv",
        "a_w_o", "kv_norm_g", "w_kv_shared", "b_pre_g", "b_post_g", "b_w_q", "b_w_o", "mlp_pre_g",
        "mlp_post_g", "mlp_w_up", "mlp_w_down"]


def kernel(**inputs):
    import concourse.bacc as _bacc
    from concourse.bass_utils import run_bass_kernel_spmd as _run

    nc = _bacc.Bacc("TRN2", target_bir_lowering=False, num_devices=1)
    arrays, args = {}, []
    for name in _INS:
        a = np.ascontiguousarray(inputs[name])
        arrays[f"in_{name}"] = a
        args.append(nc.dram_tensor(f"in_{name}", a.shape, mybir.dt.from_np(a.dtype), kind="ExternalInput").ap())
    c = shape_constants()
    arrays["shape_constants"] = c
    args.append(nc.dram_tensor("shape_constants", c.shape, F32, kind="ExternalInput").ap())
    args.append(nc.dram_tensor("out", (1, SEQ, D), F32, kind="ExternalOutput").ap())
    trunk(nc, *args)
    r = _run(nc, [arrays], core_ids=[0])
    return r.results[0]["out"]
```

```python
from contextlib import ExitStack

import numpy as np

import concourse.bass as bass
from concourse import mybir

F32 = mybir.dt.float32
F32R = mybir.dt.float32r
ALU = mybir.AluOpType
ACT = mybir.ActivationFunctionType
AX_X = mybir.AxisListType.X

P = 128
SEQ = 256
TB = SEQ // P
D = 2048
KT = D // P
HEADS = 16
NOPE = 128
ROPE = 64
LORA = 512
LT = LORA // P
D_FF = 4 * D
FFN_PARTS = D_FF // D
EPS = 1e-6
MLA_SCALE = float(NOPE + ROPE) ** -0.5
STICK_SCALE = float(P) ** -0.5

NCOL = 512
PIECE = 2 * NCOL
RAW_SLOTS = 4
PIECE_SLOTS = 4
BANKS = 8

UNIT_CHUNKS = (D // NCOL) * (D // (4 * P))
UNIT_PIECES = 2 * UNIT_CHUNKS
GROUP_PIECES = KT // 2
FEATURE_BANKS = D // P
TOKEN_BANKS = (D // NCOL) * TB
TURN_BANKS = KT // 2

STAGES = [
    ("turn_gains", 0, 1),
    ("turn_mla", 0, TURN_BANKS),
    ("latents", 2 * 4, 2 * TB),
    ("spread_mla", 0, 1),
    ("k_rope", 1, 1),
    ("turn_q_latent", 0, LT // 2),
    ("q_mla", 2, 3 * 2),
    ("turn_kv_latent", 0, LT // 2),
    ("q_mla_rest", HEADS // 2 - 2, 3 * (HEADS // 2 - 2)),
    ("kv_mla", HEADS // 2, 4 * HEADS // 2),
    ("mla", 0, 3 * HEADS),
    ("mla_out", UNIT_CHUNKS, TOKEN_BANKS),
    ("turn_mlp0", 0, TURN_BANKS),
    ("mlp0", 2 * UNIT_CHUNKS * FFN_PARTS, (FEATURE_BANKS + TOKEN_BANKS) * FFN_PARTS),
    ("turn_kv", 0, TURN_BANKS),
    ("k_shared", UNIT_CHUNKS, FEATURE_BANKS),
    ("spread_kv", 0, 1),
    ("v_shared", UNIT_CHUNKS, TOKEN_BANKS),
    ("turn_q", 0, TURN_BANKS),
    ("q_stick", UNIT_CHUNKS, FEATURE_BANKS),
    ("stick", 0, 2 * HEADS),
    ("stick_out", UNIT_CHUNKS, TOKEN_BANKS),
    ("turn_mlp1", 0, TURN_BANKS),
    ("mlp1", 2 * UNIT_CHUNKS * FFN_PARTS, (FEATURE_BANKS + TOKEN_BANKS) * FFN_PARTS),
]
CHUNK0, BANK0 = {}, {}
_c = _b = 0
for _name, _chunks, _banks in STAGES:
    CHUNK0[_name], BANK0[_name] = _c, _b
    _c, _b = _c + _chunks, _b + _banks
CHUNKS = _c
PIECES = 2 * CHUNKS
BANK_END = {name: BANK0[name] + banks for name, _, banks in STAGES}
MLP_CHUNKS = 2 * UNIT_CHUNKS
MLP_PIECES = 2 * MLP_CHUNKS
MLP_BANKS = FEATURE_BANKS + TOKEN_BANKS
assert MLP_CHUNKS % RAW_SLOTS == 0 and MLP_PIECES % PIECE_SLOTS == 0 and MLP_BANKS % BANKS == 0

USED = []
_used = 0
for _name, _chunks, _banks in STAGES:
    _units = [(2 * _chunks, _banks)]
    if _name.startswith("mlp"):
        _units = [(UNIT_PIECES, FEATURE_BANKS), (UNIT_PIECES, TOKEN_BANKS)] * FFN_PARTS
    _s = BANK0[_name]
    for _pieces, _banks in _units:
        _group = 2 if _name in ("k_rope", "q_mla", "q_mla_rest", "kv_mla") else GROUP_PIECES
        for _p in range(_pieces):
            if _p % _group == _group - 1:
                _s += _banks // (_pieces // _group)
                USED.append(("bank_full", _s))
            else:
                _used += 1
                USED.append(("piece_used", _used))
MLP_USED = MLP_PIECES - MLP_PIECES // GROUP_PIECES
assert len(USED) == PIECES

NORMS = [("pre_mla", TB, 2), ("q_latent", TB, 1), ("kv_latent", TB, 1)]
for _post, _pre in (("post_mla", "pre_mlp0"), ("post_mlp0", "pre_kv"), ("post_stick", "pre_mlp1"),
                    ("post_mlp1", None)):
    NORMS.append((_post, TB, D // NCOL))
    if _pre:
        NORMS.append((_pre, TB, 2))
REQUEST, STAT, SQUARES = {}, {}, {}
_col = _part = 0
for _i, (_name, _cols, _parts) in enumerate(NORMS):
    REQUEST[_name], STAT[_name], SQUARES[_name] = _i, _col, _part
    _col, _part = _col + _cols, _part + _cols * _parts
STATS = _col
QUARTERS = D // NCOL
POST = ["post_mla", "post_mlp0", "post_stick", "post_mlp1"]
RESIDUAL = {n: i * QUARTERS * TB for i, n in enumerate(POST)}
GAINED = {n: i * (QUARTERS - 1) * TB for i, n in enumerate(POST)}
POST_GAIN_LOADS = {n: i + 1 for i, n in enumerate(POST)}
PRE_GAINS = ["turn_mla", "turn_mlp0", "turn_kv", "turn_q", "turn_mlp1"]

FIRST_SPLITS = [3, 4, 6, 7]
CQ, CKV = KT - 2 * LT, KT - LT

IDENT, CAUSAL, STRICT, SUFFIX, LATER, COS, SIN, ONES = 0, 128, 512, 640, 768, 896, 1152, 1408
CONST_COLS = 1536

MLA_BANK, STICK_BANK = {}, {}
_n, _m = BANK0["mla"], BANK0["stick"]
for _t in range(HEADS + 2):
    for _what, _lag in (("scores", 0), ("out", 2), ("turned", 1)):
        if 0 <= _t - _lag < HEADS:
            MLA_BANK[_what, _t - _lag] = _n
            _n += 1
    for _what, _lag in (("logits", 1), ("out", 2)):
        if 0 <= _t - _lag < HEADS:
            STICK_BANK[_what, _t - _lag] = _m
            _m += 1

TURN_AHEAD = 4
BANK_ID = [s % BANKS for s in range(sum(banks for _, _, banks in STAGES))]
for _name, _next in (("mla", "mla_out"), ("stick", "stick_out")):
    for _s in range(BANK0[_name], BANK_END[_name]):
        BANK_ID[_s] = (BANK0[_next] + TB + (_s - BANK0[_name]) % (BANKS - TB)) % BANKS
for _turn in ("turn_mlp0", "turn_kv", "turn_q", "turn_mlp1"):
    for _s in range(BANK0[_turn], BANK_END[_turn]):
        BANK_ID[_s] = (BANK_END[_turn] + 4 + (_s - BANK0[_turn]) % TURN_AHEAD) % BANKS
BEFORE, _last = [], {}
for _s, _id in enumerate(BANK_ID):
    BEFORE.append(_last.get(_id))
    _last[_id] = _s
FILL_LAG = 6
FILLED = (HEADS + 2 - FILL_LAG) // 2
assert FILLED < GROUP_PIECES


def shape_constants():
    c = np.zeros((P, CONST_COLS), np.float32)
    row, col = np.arange(P)[:, None], np.arange(P)[None, :]
    c[:, IDENT:IDENT + P] = row == col
    tri = np.where(col <= row, 0.0, -1e30)
    c[:, CAUSAL:CAUSAL + P] = tri
    c[:, CAUSAL + 2 * P:CAUSAL + 3 * P] = tri
    c[:, STRICT:STRICT + P] = row < col
    c[:, SUFFIX:SUFFIX + P] = np.where(row >= col, -1.0, 0.0)
    c[:, LATER:LATER + P] = -1.0
    c[:, ONES:ONES + P] = 1.0
    half = ROPE // 2
    inv = np.float32(10000.0) ** (-np.arange(0, ROPE, 2, dtype=np.float32) / np.float32(ROPE))
    ang = (np.arange(SEQ, dtype=np.float32)[:, None] * inv[None, :]).astype(np.float32)
    cos, sin = np.cos(ang).T, np.sin(ang).T
    for q in range(P // half):
        c[q * half:(q + 1) * half, COS:COS + SEQ] = cos
        c[q * half:(q + 1) * half, SIN:SIN + SEQ] = -sin if q % 2 == 0 else sin
    return c


def trunk(nc, x, a_pre_g, a_post_g, w_lat, q_norm_g, kv_norm_g, w_uq, w_ukv, w_mla_o, kv_g, w_kv,
          b_pre_g, b_post_g, w_q, w_stick_o, mlp_pre_g, mlp_post_g, w_up, w_down, consts, out):
    ctx = ExitStack()
    with ctx:
        def sb(name, shape, dt=F32):
            return ctx.enter_context(nc.sbuf_tensor(name, shape, dt))

        def sem(name):
            return ctx.enter_context(nc.semaphore(name))

        resid = sb("resid", [P, TB, D])
        branch = sb("branch", [P, TB, D])
        xT = sb("xT", [P, KT, 2, SEQ], F32R)
        with nc.sbuf_tensor("hidT", [P, KT, 2, SEQ], F32R) as hidT:
            pass
        keyT = sb("keyT", [P, HEADS, SEQ])
        val = sb("val", [P, TB, HEADS * P])
        raw = sb("raw", [P, RAW_SLOTS, 2 * PIECE])
        whi = sb("whi", [P, PIECE_SLOTS, PIECE], F32R)
        wlo = sb("wlo", [P, PIECE_SLOTS, PIECE], F32R)
        gain_post = sb("gain_post", [P, D])
        gain_latent = sb("gain_latent", [P, 2 * LORA])
        gain_rows = sb("gain_rows", [len(PRE_GAINS) * KT, P])
        gainT = sb("gainT", [P, len(PRE_GAINS) * KT])
        rms_diag = sb("rms_diag", [P, TB, P])
        spread = sb("spread", [P, SEQ])
        with nc.sbuf_tensor("junk", [P, D], F32) as junk:
            pass
        with nc.sbuf_tensor("soft", [P, 4, 384], F32) as soft:
            pass
        qropeT = sb("qropeT", [P, HEADS // 2, SEQ])
        kropeT = sb("kropeT", [P, SEQ])
        work = sb("work", [P, 12, SEQ])
        con = sb("con", [P, CONST_COLS])
        squares = sb("squares", [P, STATS, QUARTERS])
        stat = sb("stat", [P, 4, STATS])
        power = sb("power", [P, 2 * TB])
        rows = sb("rows", [P, 3, 2 * HEADS])
        queryT = branch.rearrange("p b (h t) -> p (b h) t", t=SEQ)
        latents = [branch[:, :, 0:LORA], val[:, :, 0:LORA]]
        bank = ctx.enter_context(nc.psum_tensor("bank", [P, BANKS, 512], F32))

        half_sum, full_sum = work[:, 0:4, :], work[:, 4:8, :]
        pairs = work.rearrange("p a t -> p (a t)")
        probs = pairs[:, 0:768].rearrange("p (b n) -> p b n", b=2)
        probsT = pairs[:, 768:1536].rearrange("p (b n) -> p b n", b=2)

        ident = con[:, IDENT:IDENT + P]
        strict2 = con[:, STRICT:STRICT + P].unsqueeze(1).to_broadcast([P, 2, P])

        raw_loaded = [sem(f"raw_loaded{i}") for i in range(RAW_SLOTS)]
        hi_ready, lo_ready, piece_used = sem("hi_ready"), sem("lo_ready"), sem("piece_used")
        bank_full, bank_free = sem("bank_full"), sem("bank_free")
        x_loaded = [sem(f"x_loaded{b}") for b in range(TB)]
        ident_loaded, con_loaded, out_stored = sem("ident_loaded"), sem("con_loaded"), sem("out_stored")
        gain_rows_loaded, latent_gain_loaded = sem("gain_rows_loaded"), sem("latent_gain_loaded")
        post_gain_loaded = sem("post_gain_loaded")
        power_set, branch_zeroed = sem("power_set"), sem("branch_zeroed")
        squares_ready, sum_ready = sem("squares_ready"), sem("sum_ready")
        mean_ready, rms_ready = sem("mean_ready"), sem("rms_ready")
        gain_scaled, last_scaled, resid_ready = sem("gain_scaled"), sem("last_scaled"), sem("resid_ready")
        square_ready, diag_ready, rms_applied = sem("square_ready"), sem("diag_ready"), sem("rms_applied")
        latent_normed, turned_hi = sem("latent_normed"), sem("turned_hi")
        half_ready, relu2_ready = sem("half_ready"), sem("relu2_ready")
        hidden_hi, hidden_ready = sem("hidden_hi"), sem("hidden_ready")
        swapped_low, swapped_high = sem("swapped_low"), sem("swapped_high")
        rope_terms, rope_ready = sem("rope_terms"), sem("rope_ready")
        row_max, exp_ready, sum_inverse = sem("row_max"), sem("exp_ready"), sem("sum_inverse")
        probs_ready, out_hi = sem("probs_ready"), sem("out_hi")
        logit_ready, abs_ready, exp_abs, log_term = sem("logit_ready"), sem("abs_ready"), sem("exp_abs"), sem("log_term")
        softplus, masked_softplus = sem("softplus"), sem("masked_softplus")
        stick_exp, stick_ready = sem("stick_exp"), sem("stick_ready")

        def q_bank(i):
            return BANK0["q_mla"] + 3 * i if i < 2 else BANK0["q_mla_rest"] + 3 * (i - 2)

        def bank_of(s):
            return bank[:, BANK_ID[s], :]

        def split_moves(p):
            q = p % PIECE_SLOTS
            if p // 2 == CHUNK0["k_rope"]:
                src = raw[:, (p // 2) % RAW_SLOTS, (p % 2) * NCOL:(p % 2 + 1) * NCOL]
                src = src.rearrange("p (k n) -> p k n", n=ROPE)
                hi, lo = (w[:, q, :].rearrange("p (k d n) -> p k d n", d=2, n=ROPE) for w in (whi, wlo))
                return [(src, hi[:, :, d, :], lo[:, :, d, :]) for d in range(2)]
            if CHUNK0["q_mla"] <= p // 2 < CHUNK0["kv_mla"]:
                n = 2 * 2 * (NOPE + ROPE)
                src = raw[:, (p // 2) % RAW_SLOTS, (p % 2) * n:(p % 2 + 1) * n]
                src = src.rearrange("p (k h n) -> p k h n", k=2, h=2)
                hi, lo = (w[:, q, 0:n].rearrange("p (k n) -> p k n", k=2) for w in (whi, wlo))
                out = []
                for c0, c1, d0 in ((0, NOPE, 0), (NOPE, NOPE + ROPE, 2 * NOPE)):
                    d1 = d0 + 2 * (c1 - c0)
                    out.append((src[:, :, :, c0:c1], *(w[:, :, d0:d1].rearrange("p k (h n) -> p k h n", h=2)
                                                       for w in (hi, lo))))
                return out
            return [(raw[:, (p // 2) % RAW_SLOTS, (p % 2) * PIECE:(p % 2 + 1) * PIECE], whi[:, q, :], wlo[:, q, :])]

        HALF = {"k_rope": 0, "q_mla": 1, "kv_mla": 1 + 3 * HEADS // 2}
        HALF["mlp0"] = HALF["kv_mla"] + HEADS
        HALF["k_shared"] = HALF["mlp0"] + FEATURE_BANKS * FFN_PARTS
        HALF["q_stick"] = HALF["k_shared"] + FEATURE_BANKS
        HALF["mlp1"] = HALF["q_stick"] + FEATURE_BANKS
        HIDDEN = {"mlp0": 0, "mlp1": FEATURE_BANKS * FFN_PARTS}
        TURN, n = {}, 0
        for name, _, banks in STAGES:
            if name.startswith("turn") and name != "turn_gains":
                TURN[name], n = n, n + banks
        KEY_SCALED, QUERY_SCALED = 1, 1 + HEADS
        ZEROED = {"mlp0": 1, "mlp1": 2}
        BRANCH_BANK = {"post_mla": BANK0["mla_out"], "post_mlp0": BANK_END["mlp0"] - TOKEN_BANKS,
                       "post_stick": BANK0["stick_out"], "post_mlp1": BANK_END["mlp1"] - TOKEN_BANKS}

        block = ctx.enter_context(nc.Block())

        @block.sync
        def _(sp):
            def load_chunk(c, off, dst, src):
                if c >= RAW_SLOTS:
                    sp.wait_ge(lo_ready, 2 * (c - RAW_SLOTS) + 2 + off * 2)
                sp.dma_start(dst, src).then_inc(raw_loaded[c % RAW_SLOTS], 16)

            def raw_chunk(c, k, n):
                return raw[:, c % RAW_SLOTS, 0:k * n].rearrange("p (k n) -> p k n", k=k)

            def load_unit(c0, off, w, row0, col0):
                wv = w.rearrange("(k p) n -> p k n", p=P)
                for i in range(UNIT_CHUNKS):
                    g, kc = divmod(i, KT // 4)
                    load_chunk(c0 + i, off, raw_chunk(c0 + i, 4, NCOL),
                               wv[:, bass.ds(row0 + 4 * kc, 4), bass.ds(col0 + g * NCOL, NCOL)])

            sp.dma_start(con[:, IDENT:IDENT + P], consts[:, IDENT:IDENT + P]).then_inc(ident_loaded, 16)
            for b in range(TB):
                sp.dma_start(resid[:, b, :], x[0, b * P:(b + 1) * P, :]).then_inc(x_loaded[b], 16)
            for n, g in enumerate((a_pre_g[0], mlp_pre_g[0], kv_g, b_pre_g[0], mlp_pre_g[1])):
                sp.dma_start(gain_rows[n * KT:(n + 1) * KT, :],
                             g.rearrange("(k p) -> k p", p=P)).then_inc(gain_rows_loaded, 16)
            c = CHUNK0["latents"]
            wv = w_lat[0].rearrange("(k p) n -> p k n", p=P)
            for i in range(8):
                g, kc = divmod(i, 4)
                load_chunk(c + i, 0, raw_chunk(c + i, 4, NCOL),
                           wv[:, 4 * kc:4 * kc + 4, g * NCOL:(g + 1) * NCOL])
            sp.dma_start(con[:, IDENT + P:], consts[:, IDENT + P:]).then_inc(con_loaded, 16)
            c = CHUNK0["k_rope"]
            load_chunk(c, 0, raw_chunk(c, KT, ROPE), wv[:, :, 2 * LORA:2 * LORA + ROPE])
            c = CHUNK0["q_mla"]
            wv = w_uq[0].rearrange("(k p) n -> p k n", p=P)
            for i in range(HEADS // 2):
                n2 = 2 * (NOPE + ROPE)
                load_chunk(c + i, 0, raw_chunk(c + i, LT, n2), wv[:, :, i * n2:(i + 1) * n2])
            c = CHUNK0["kv_mla"]
            wv = w_ukv[0].rearrange("(k p) n -> p k n", p=P)
            for i in range(HEADS // 2):
                load_chunk(c + i, 0, raw_chunk(c + i, LT, NCOL), wv[:, :, i * NCOL:(i + 1) * NCOL])
            load_unit(CHUNK0["mla_out"], 0, w_mla_o[0], 0, 0)

            def load_mlp(name, layer):
                with sp.Fori(0, FFN_PARTS) as part:
                    c0 = CHUNK0[name]
                    load_unit(c0, part * MLP_CHUNKS, w_up[layer], 0, part * D)
                    load_unit(c0 + UNIT_CHUNKS, part * MLP_CHUNKS, w_down[layer], part * KT, 0)

            load_mlp("mlp0", 0)
            load_unit(CHUNK0["k_shared"], 0, w_kv, 0, 0)
            load_unit(CHUNK0["v_shared"], 0, w_kv, 0, D)
            load_unit(CHUNK0["q_stick"], 0, w_q[0], 0, 0)
            load_unit(CHUNK0["stick_out"], 0, w_stick_o[0], 0, 0)
            load_mlp("mlp1", 1)
            for q in range(QUARTERS):
                cols = slice(q * NCOL, (q + 1) * NCOL)
                sp.wait_ge(resid_ready, RESIDUAL["post_mlp1"] + TB * (q + 1))
                sp.dma_start(out[0].rearrange("(b p) n -> p b n", p=P)[:, :, cols],
                             resid[:, :, cols]).then_inc(out_stored, 16)
            sp.wait_ge(out_stored, 16 * QUARTERS)

        @block.gpsimd
        def _(pool):
            def load_gain(tile, g, loaded):
                pool.dma_start(tile, g.partition_broadcast(P)).then_inc(loaded, 16)

            def inverse_rms(name, width):
                r, i = REQUEST[name], STAT[name]
                n = NORMS[r][1]
                pool.wait_ge(sum_ready, r + 1)
                nc.gpsimd.tensor_scalar(stat[:, 1, i:i + n], stat[:, 0, i:i + n], 1.0 / width, EPS,
                                        ALU.mult, ALU.add).then_inc(mean_ready, 1)
                pool.wait_ge(mean_ready, r + 1)
                nc.gpsimd.tensor_tensor(stat[:, 2, i:i + n], stat[:, 1, i:i + n], power[:, 0:n],
                                        ALU.pow).then_inc(rms_ready, 1)

            def square_rms(name):
                i = STAT[name]
                pool.wait_ge(rms_ready, REQUEST[name] + 1)
                nc.gpsimd.tensor_tensor(stat[:, 3, i:i + TB], stat[:, 2, i:i + TB], stat[:, 2, i:i + TB],
                                        ALU.mult).then_inc(square_ready, 1)

            def diagonal(name):
                for b in range(TB):
                    i = STAT[name] + b
                    pool.wait_ge(rms_ready, REQUEST[name] + 1)
                    nc.gpsimd.tensor_scalar(rms_diag[:, b, :], ident, stat[:, 2, i:i + 1], None,
                                            ALU.mult).then_inc(diag_ready, 1)

            def apply_rms(dst, s):
                pool.wait_ge(bank_free, s + 1)
                nc.gpsimd.tensor_tensor(dst, dst, spread[:, :], ALU.mult).then_inc(rms_applied, 1)

            def scale_by_gain(name):
                pool.wait_ge(post_gain_loaded, 16 * POST_GAIN_LOADS[name])
                for g in range(QUARTERS - 1):
                    for b in range(TB):
                        cols = slice(g * NCOL, (g + 1) * NCOL)
                        pool.wait_ge(squares_ready, SQUARES[name] + TB * g + b + 1)
                        nc.gpsimd.tensor_tensor(branch[:, b, cols], branch[:, b, cols], gain_post[:, cols],
                                                ALU.mult).then_inc(gain_scaled, 1)

            def zero_branch(post):
                pool.wait_ge(resid_ready, RESIDUAL[post] + all_updates)
                nc.gpsimd.memset(branch[:, :, :], 0.0).then_inc(branch_zeroed, 1)

            def rotate(dst, s, n):
                u, w = full_sum[:, 2 * (n % 2), :], full_sum[:, 2 * (n % 2) + 1, :]
                pool.wait_ge(bank_free, s + 1)
                nc.gpsimd.tensor_tensor(dst, u, con[:, COS:COS + SEQ], ALU.mult).then_inc(rope_terms, 1)
                pool.wait_ge(swapped_low, 2 * (n + 1))
                pool.wait_ge(swapped_high, 2 * (n + 1))
                nc.gpsimd.tensor_tensor(w, w, con[:, SIN:SIN + SEQ], ALU.mult).then_inc(rope_terms, 1)
                pool.wait_ge(rope_terms, 2 * (n + 1))
                nc.gpsimd.tensor_tensor(dst, dst, w, ALU.add).then_inc(rope_ready, 1)

            all_updates = QUARTERS * TB
            nc.gpsimd.memset(power[:, :], -0.5).then_inc(power_set, 1)
            pool.wait_ge(power_set, 1)
            inverse_rms("pre_mla", D)
            pool.wait_ge(ident_loaded, 16)
            diagonal("pre_mla")
            load_gain(gain_latent[:, 0:LORA], q_norm_g[0], latent_gain_loaded)
            load_gain(gain_latent[:, LORA:2 * LORA], kv_norm_g[0], latent_gain_loaded)
            load_gain(gain_post[:, :], a_post_g[0], post_gain_loaded)
            inverse_rms("q_latent", LORA)
            pool.wait_ge(con_loaded, 16)
            rotate(kropeT[:, :], BANK0["k_rope"], 0)
            pool.wait_ge(rope_ready, 1)
            apply_rms(kropeT[:, :], BANK0["spread_mla"])
            inverse_rms("kv_latent", LORA)
            for i in range(HEADS // 2):
                rotate(qropeT[:, i, :], q_bank(i) + 2, 1 + i)
            scale_by_gain("post_mla")
            inverse_rms("post_mla", D)
            zero_branch("post_mla")
            load_gain(gain_post[:, :], mlp_post_g[0], post_gain_loaded)
            inverse_rms("pre_mlp0", D)
            square_rms("pre_mlp0")
            scale_by_gain("post_mlp0")
            inverse_rms("post_mlp0", D)
            pool.wait_ge(last_scaled, TB * 2)
            load_gain(gain_post[:, :], b_post_g[0], post_gain_loaded)
            inverse_rms("pre_kv", D)
            pool.wait_ge(bank_free, BANK0["spread_mla"] + 1)
            diagonal("pre_kv")
            for k in range(HEADS):
                apply_rms(keyT[:, k, :], BANK0["spread_kv"])
            for k in range(HEADS):
                apply_rms(queryT[:, k, :], BANK0["q_stick"] + k)
            for t in range(HEADS):
                pool.wait_ge(stick_exp, t + 1)
                diag = probs[:, t % 2, :].rearrange("p (b n) -> p b n", b=3)[:, 0:3:2, :]
                nc.gpsimd.tensor_tensor(diag, diag, strict2, ALU.mult).then_inc(stick_ready, 1)
            scale_by_gain("post_stick")
            inverse_rms("post_stick", D)
            zero_branch("post_stick")
            load_gain(gain_post[:, :], mlp_post_g[1], post_gain_loaded)
            inverse_rms("pre_mlp1", D)
            square_rms("pre_mlp1")
            scale_by_gain("post_mlp1")
            inverse_rms("post_mlp1", D)

        @block.scalar
        def _(act):
            def split_hi(p, part=0):
                if p % 2 == 0:
                    c = p // 2
                    act.wait_ge(raw_loaded[c % RAW_SLOTS],
                                16 * (c // RAW_SLOTS + 1) + part * (16 * MLP_CHUNKS // RAW_SLOTS))
                moves = split_moves(p)
                for src, hi, lo in moves[:-1]:
                    nc.scalar.activation(hi, src, ACT.Copy)
                src, hi, lo = moves[-1]
                nc.scalar.activation(hi, src, ACT.Copy).then_inc(hi_ready, 1)

            def split_ahead(p, part=0):
                if p + PIECE_SLOTS < PIECES:
                    signal, value = USED[p]
                    if signal == "bank_full":
                        act.wait_ge(bank_full, value + part * MLP_BANKS)
                    else:
                        act.wait_ge(piece_used, value + part * MLP_USED)
                    split_hi(p + PIECE_SLOTS, part)

            def sum_squares(n, col, src):
                if n:
                    act.wait_ge(squares_ready, n)
                nc.scalar.activation(junk[:, 0:src.shape[-1]], src, ACT.Square,
                                     accum_out=col).then_inc(squares_ready, 1)

            def branch_squares(name, g):
                for b in range(TB):
                    act.wait_ge(bank_free, BRANCH_BANK[name] + TB * g + b + 1)
                    sum_squares(SQUARES[name] + TB * g + b,
                                squares[:, STAT[name] + b, g:g + 1],
                                branch[:, b, g * NCOL:(g + 1) * NCOL])

            def resid_squares(name, b, h):
                sum_squares(SQUARES[name] + TB * h + b, squares[:, STAT[name] + b, h:h + 1],
                            resid[:, b, h * D // 2:(h + 1) * D // 2])

            def turn_hi(name, i, k0=0):
                s = BANK0[name] + i
                act.wait_ge(bank_full, s + 1)
                if name not in PRE_GAINS:
                    nc.scalar.activation(xT[:, k0 + 2 * i:k0 + 2 * i + 2, 0, :],
                                         bank_of(s).rearrange("p (k t) -> p k t", k=2),
                                         ACT.Copy).then_inc(turned_hi, 1)
                    return
                g = PRE_GAINS.index(name) * KT
                for k, last in ((2 * i, False), (2 * i + 1, True)):
                    hi = nc.scalar.activation(xT[:, k, 0, :], bank_of(s)[:, (k % 2) * SEQ:(k % 2 + 1) * SEQ],
                                              ACT.Copy, scale=gainT[:, g + k:g + k + 1])
                    if last:
                        hi.then_inc(turned_hi, 1)

            def turn_stage(name, p0, post=None, pre=None):
                for i in range(TURN_BANKS):
                    if i == 2:
                        split_ahead(p0 - 1)
                    if i >= TURN_BANKS - 2:
                        split_ahead(p0 + i - (TURN_BANKS - 2))
                    turn_hi(name, i)
                    if pre and 3 <= i < 7:
                        h, b = divmod(i - 3, 2)
                        act.wait_ge(resid_ready, RESIDUAL[post] + TB * 2 * (h + 1))
                        resid_squares(pre, b, h)

            def take_half(s, off, i, scale=1.0, before=None):
                if before is not None:
                    act.wait_ge(bank_free, before + 1)
                act.wait_ge(bank_full, s + 1 + off)
                nc.scalar.activation(half_sum[:, i % 4, :], bank_of(s)[:, SEQ:2 * SEQ], ACT.Copy,
                                     scale=scale).then_inc(half_ready, 1)

            def swap_rope(s, n):
                act.wait_ge(bank_free, s + 1)
                for q in (2, 3):
                    src = full_sum[32 * (q ^ 1):32 * (q ^ 1) + 32, 2 * (n % 2), :]
                    nc.scalar.activation(full_sum[32 * q:32 * q + 32, 2 * (n % 2) + 1, :], src,
                                         ACT.Copy).then_inc(swapped_high, 1)

            def feature_stage(name, scale, first=0, before_last=None):
                for i in range(first, UNIT_PIECES):
                    if before_last and i == UNIT_PIECES - 1:
                        before_last()
                    if i % GROUP_PIECES == GROUP_PIECES - 1:
                        for f in range(4):
                            s = BANK0[name] + i // GROUP_PIECES * 4 + f
                            take_half(s, 0, f, scale, before=s - 4 if i >= GROUP_PIECES else None)
                    split_ahead(2 * CHUNK0[name] + i)

            def token_stage(name, norm=None, p0=None, part=0, last=False, first=0, hold=False):
                p0 = 2 * CHUNK0[name] if p0 is None else p0
                for i in range(first, UNIT_PIECES):
                    if i < UNIT_PIECES - (PIECE_SLOTS if last else 1 if norm or hold else 0):
                        split_ahead(p0 + i, part)
                    if norm and i >= GROUP_PIECES and i % GROUP_PIECES == 1:
                        branch_squares(norm, i // GROUP_PIECES - 1)
                if norm:
                    branch_squares(norm, QUARTERS - 1)

            def fill_ahead(name, step):
                k = (step - FILL_LAG - 2) // 2
                if step % 2 == 0 and k >= 0:
                    split_ahead(2 * CHUNK0[name] + k)

            act.wait_ge(bank_free, BANK_END["turn_gains"])
            for i in range(TURN_BANKS):
                turn_hi("turn_mla", i)
                if i in FIRST_SPLITS:
                    split_hi(FIRST_SPLITS.index(i))
            for b in range(TB):
                act.wait_ge(x_loaded[b], 16)

            def latent_squares(name, g):
                for b in range(TB):
                    act.wait_ge(bank_free, BANK0["latents"] + TB * g + b + 1)
                    sum_squares(SQUARES[name] + b, squares[:, STAT[name] + b, 0:1],
                                latents[g][:, b, :])

            for i in range(2 * GROUP_PIECES):
                split_ahead(2 * CHUNK0["latents"] + i)
                if i < 2 * TB:
                    resid_squares("pre_mla", i % TB, i // TB)
                if i == GROUP_PIECES:
                    latent_squares("q_latent", 0)
            latent_squares("kv_latent", 1)
            take_half(BANK0["k_rope"], 0, 0)
            swap_rope(BANK0["k_rope"], 0)
            for i in range(LT // 2):
                turn_hi("turn_q_latent", i, CQ)
            for i in range(2):
                split_ahead(2 * CHUNK0["k_rope"] + i)
            for i in range(HEADS // 2):
                s = q_bank(i)
                split_ahead(2 * (CHUNK0["q_mla"] + i))
                for f in range(3):
                    take_half(s + f, 0, f, MLA_SCALE, before=q_bank(i - 1) + f if i else None)
                split_ahead(2 * (CHUNK0["q_mla"] + i) + 1)
                swap_rope(s + 2, 1 + i)
                if i == 1:
                    for j in range(LT // 2):
                        turn_hi("turn_kv_latent", j, CKV)
            for i in range(HEADS // 2):
                s = BANK0["kv_mla"] + 4 * i
                split_ahead(2 * (CHUNK0["kv_mla"] + i))
                for f in range(2):
                    take_half(s + f, 0, f, before=s + f - 4 if i else None)
                split_ahead(2 * (CHUNK0["kv_mla"] + i) + 1)

            def out_split(t, s):
                act.wait_ge(bank_full, s + 1)
                nc.scalar.activation(xT[:, t, 0, :], bank_of(s)[:, 0:SEQ], ACT.Copy).then_inc(out_hi, 1)

            for step in range(HEADS + 2):
                if 1 <= step <= HEADS:
                    t = step - 1
                    act.wait_ge(sum_inverse, t + 1)
                    for q, (c0, c1) in enumerate(((0, P), (P, 3 * P))):
                        i = 2 * t + q
                        nc.scalar.activation(probs[:, t % 2, c0:c1], probs[:, t % 2, c0:c1], ACT.Copy,
                                             scale=rows[:, 2, i:i + 1]).then_inc(probs_ready, 1)
                if step < HEADS:
                    t = step
                    act.wait_ge(row_max, 2 * t + 2)
                    for q, (c0, c1) in enumerate(((0, P), (P, 3 * P))):
                        i = 2 * t + q
                        nc.scalar.activation(probs[:, t % 2, c0:c1], probs[:, t % 2, c0:c1], ACT.Exp,
                                             bias=rows[:, 0, i:i + 1],
                                             accum_out=rows[:, 1, i:i + 1]).then_inc(exp_ready, 1)
                if step >= 2:
                    out_split(step - 2, MLA_BANK["out", step - 2])
                fill_ahead("mla_out", step)
            token_stage("mla_out", "post_mla", first=FILLED - 1)
            turn_stage("turn_mlp0", 2 * CHUNK0["mlp0"], "post_mla", "pre_mlp0")

            def mlp_part(name, part, norm=None, last=False, first=0):
                p0, s0 = 2 * CHUNK0[name], BANK0[name]
                soff, foff = part * MLP_BANKS, part * FEATURE_BANKS
                for i in range(first, UNIT_PIECES):
                    if i % GROUP_PIECES == GROUP_PIECES - 1:
                        g = i // GROUP_PIECES
                        for f in range(5):
                            if f < 4:
                                take_half(s0 + 4 * g + f, soff, f)
                            if f >= 1:
                                k = 4 * g + f - 1
                                act.wait_ge(relu2_ready, HIDDEN[name] + k + 1 + foff)
                                nc.scalar.activation(hidT[:, k, 0, :], full_sum[:, k % 4, :],
                                                     ACT.Copy).then_inc(hidden_hi, 1)
                    split_ahead(p0 + i, part)
                token_stage(name, norm, p0 + UNIT_PIECES, part, last)

            mlp_part("mlp0", 0, first=2)
            with act.Fori(1, FFN_PARTS - 1) as part:
                mlp_part("mlp0", part)
            mlp_part("mlp0", FFN_PARTS - 1, "post_mlp0")
            turn_stage("turn_kv", 2 * CHUNK0["k_shared"], "post_mlp0", "pre_kv")

            feature_stage("k_shared", 1.0, first=2)
            token_stage("v_shared", hold=True)
            turn_stage("turn_q", 2 * CHUNK0["q_stick"])

            def softplus_tail(t):
                tail = soft[:, t % 2, :]
                act.wait_ge(logit_ready, t + 1)
                nc.scalar.activation(tail, bank_of(STICK_BANK["logits", t])[:, 0:384],
                                     ACT.Abs).then_inc(abs_ready, 1)
                act.wait_ge(abs_ready, t + 1)
                nc.scalar.activation(tail, tail, ACT.Exp, scale=-1.0).then_inc(exp_abs, 1)
                act.wait_ge(exp_abs, t + 1)
                nc.scalar.activation(tail, tail, ACT.Ln, bias=1.0).then_inc(log_term, 1)

            def first_tail():
                nc.scalar.preload_act_table_set("natural_log_exp_and_others")
                softplus_tail(0)

            feature_stage("q_stick", STICK_SCALE, first=2, before_last=first_tail)
            for step in range(1, HEADS + 2):
                if step < HEADS:
                    softplus_tail(step)
                if 1 <= step <= HEADS:
                    t = step - 1
                    act.wait_ge(bank_free, STICK_BANK["logits", t] + 1)
                    nc.scalar.activation(probs[:, t % 2, :], probs[:, t % 2, :], ACT.Exp).then_inc(stick_exp, 1)
                if step >= 2:
                    out_split(step - 2, STICK_BANK["out", step - 2])
                fill_ahead("stick_out", step)
            token_stage("stick_out", "post_stick", first=FILLED - 1)
            turn_stage("turn_mlp1", 2 * CHUNK0["mlp1"], "post_stick", "pre_mlp1")
            mlp_part("mlp1", 0, first=2)
            with act.Fori(1, FFN_PARTS - 1) as part:
                mlp_part("mlp1", part)
            mlp_part("mlp1", FFN_PARTS - 1, "post_mlp1", last=True)

        @block.tensor
        def _(pe):
            def open_bank(s, off=0):
                if BEFORE[s] is not None:
                    pe.wait_ge(bank_free, BEFORE[s] + 1 + off)

            def piece(p, off=0, k=2):
                pe.wait_ge(lo_ready, p + 1 + off)
                n = 2 * (NOPE + ROPE) if CHUNK0["q_mla"] <= p // 2 < CHUNK0["kv_mla"] else PIECE // k
                return [w[:, p % PIECE_SLOTS, 0:k * n].rearrange("p (k n) -> p k n", k=k) for w in (whi, wlo)]

            def feature_block(s, hi, lo, op, first, last):
                nc.tensor.matmul(bank_of(s), hi, op, start=first, stop=False)
                return nc.tensor.matmul(bank_of(s)[:, 0:SEQ], lo, op[:, 0, :], start=False, stop=last)

            def token_block(dst, hi, lo, op, b, first, last):
                t = slice(b * P, (b + 1) * P)
                nc.tensor.matmul(dst, op[:, 0, t], hi, start=first, stop=False)
                nc.tensor.matmul(dst, op[:, 0, t], lo, start=False, stop=False)
                return nc.tensor.matmul(dst, op[:, 1, t], hi, start=False, stop=last)

            def feature_unit(p0, s0, poff=0, soff=0, op=xT, ready=None, before_last=None):
                for i in range(UNIT_PIECES):
                    if before_last and i == UNIT_PIECES - 1:
                        before_last()
                    g, kp = divmod(i, GROUP_PIECES)
                    if ready and g == 0:
                        ready(kp)
                    hi, lo = piece(p0 + i, poff)
                    for f in range(4):
                        s = s0 + 4 * g + f
                        if kp == 0:
                            open_bank(s, soff)
                        for k in range(2):
                            kt = 2 * kp + k
                            mm = feature_block(s, hi[:, k, f * P:(f + 1) * P], lo[:, k, f * P:(f + 1) * P],
                                               op[:, kt, :, :], kt == 0, kt == KT - 1)
                        if kp == GROUP_PIECES - 1:
                            mm.then_inc(bank_full, 1)
                    if kp < GROUP_PIECES - 1:
                        mm.then_inc(piece_used, 1)

            def token_piece(p, s, kp, b, poff=0, soff=0, op=xT):
                hi, lo = piece(p, poff)
                if kp == 0:
                    open_bank(s, soff)
                for k in range(2):
                    kt = 2 * kp + k
                    mm = token_block(bank_of(s), hi[:, k, :], lo[:, k, :], op[:, kt, :, :], b,
                                     kt == 0, kt == KT - 1)
                if kp == GROUP_PIECES - 1:
                    mm.then_inc(bank_full, 1)
                elif b == TB - 1:
                    mm.then_inc(piece_used, 1)

            def token_unit(p0, s0, poff=0, soff=0, op=xT, groups=D // NCOL, ready=None, first=0):
                for i in range(first, groups * GROUP_PIECES):
                    g, kp = divmod(i, GROUP_PIECES)
                    if ready and g == 0:
                        ready(kp)
                    for b in range(TB):
                        token_piece(p0 + i, s0 + TB * g + b, kp, b, poff, soff, op)

            def fill(name, banks, step):
                k, b = divmod(step - FILL_LAG, 2)
                if k >= 0:
                    pe.wait_ge(bank_free, banks["out", 2 * k + 1] + 1)
                    token_piece(2 * CHUNK0[name] + k, BANK0[name] + b, k, b)

            def turn(name, i, src=resid):
                s = BANK0[name] + i
                open_bank(s)
                for j in range(4):
                    kt, b = 2 * i + j // 2, j % 2
                    mm = nc.tensor.transpose(bank_of(s)[:, j * P:(j + 1) * P],
                                             src[:, b, kt * P:(kt + 1) * P], ident)
                mm.then_inc(bank_full, 1)

            def turned(name):
                return lambda kp: pe.wait_ge(bank_free, BANK0[name] + kp + 1)

            def turning(name, post=None):
                def ready(kp):
                    for i in range(0 if kp == 0 else kp + TURN_AHEAD - 1, min(kp + TURN_AHEAD, TURN_BANKS)):
                        if post and i % 2 == 0:
                            pe.wait_ge(resid_ready, RESIDUAL[post] + TB * (i // 2 + 1))
                        turn(name, i)
                    pe.wait_ge(bank_free, BANK0[name] + kp + 1)
                return ready

            def spread_rms(name, n):
                s = BANK0[name]
                open_bank(s)
                for b in range(TB):
                    pe.wait_ge(diag_ready, TB * n + b + 1)
                    mm = nc.tensor.matmul(bank_of(s)[:, b * P:(b + 1) * P], con[:, ONES:ONES + P],
                                          rms_diag[:, b, :], start=True, stop=True)
                mm.then_inc(bank_full, 1)

            pe.wait_ge(ident_loaded, 16)
            pe.wait_ge(gain_rows_loaded, 16 * len(PRE_GAINS))
            rows_ = len(PRE_GAINS) * KT
            nc.tensor.transpose(bank_of(BANK0["turn_gains"])[:, 0:rows_], gain_rows[:, :],
                                con[0:rows_, IDENT:IDENT + rows_]).then_inc(bank_full, 1)
            for b in range(TB):
                pe.wait_ge(x_loaded[b], 16)
            for i in range(TURN_BANKS):
                turn("turn_mla", i)
            token_unit(2 * CHUNK0["latents"], BANK0["latents"], groups=2, ready=turned("turn_mla"))
            pe.wait_ge(con_loaded, 16)
            spread_rms("spread_mla", 0)
            s = BANK0["k_rope"]
            open_bank(s)
            for i in range(2):
                hi, lo = piece(2 * CHUNK0["k_rope"] + i, k=KT // 2)
                for k in range(KT // 2):
                    kt = i * KT // 2 + k
                    mm = feature_block(s, hi[:, k, :], lo[:, k, :], xT[:, kt, :, :], kt == 0, kt == KT - 1)
                mm.then_inc(piece_used if i == 0 else bank_full, 1)
            pe.wait_ge(latent_normed, TB)
            for i in range(LT // 2):
                turn("turn_q_latent", i, latents[0])
            for i in range(HEADS // 2):
                s = q_bank(i)
                for j in range(2):
                    if i == 0:
                        pe.wait_ge(bank_free, BANK0["turn_q_latent"] + j + 1)
                    hi, lo = piece(2 * (CHUNK0["q_mla"] + i) + j)
                    for f in range(3):
                        if j == 0:
                            open_bank(s + f)
                        for k in range(2):
                            kt = 2 * j + k
                            cols = slice(f * P, (f + 1) * P)
                            mm = feature_block(s + f, hi[:, k, cols], lo[:, k, cols], xT[:, CQ + kt, :, :], kt == 0, kt == LT - 1)
                        if j == 1:
                            mm.then_inc(bank_full, 1)
                    if j == 0:
                        mm.then_inc(piece_used, 1)
                if i == 1:
                    pe.wait_ge(latent_normed, 2 * TB)
                    for j in range(LT // 2):
                        turn("turn_kv_latent", j, latents[1])
            for i in range(HEADS // 2):
                s = BANK0["kv_mla"] + 4 * i
                for j in range(2):
                    if i == 0:
                        pe.wait_ge(bank_free, BANK0["turn_kv_latent"] + j + 1)
                    hi, lo = piece(2 * (CHUNK0["kv_mla"] + i) + j)
                    for f in range(2):
                        if j == 0:
                            open_bank(s + f)
                        for k in range(2):
                            kt = 2 * j + k
                            cols = slice(2 * f * P, (2 * f + 1) * P)
                            mm = feature_block(s + f, hi[:, k, cols], lo[:, k, cols], xT[:, CKV + kt, :, :],
                                               kt == 0, kt == LT - 1)
                        if j == 1:
                            mm.then_inc(bank_full, 1)
                    for b in range(TB):
                        if j == 0:
                            open_bank(s + 2 + b)
                        dst = bank_of(s + 2 + b)[:, 0:2 * P]
                        for k in range(2):
                            kt = 2 * j + k
                            h, l = (w[:, k, :].rearrange("p (h n) -> p h n", n=P)[:, 1:4:2, :] for w in (hi, lo))
                            mm = token_block(dst, h, l, xT[:, CKV + kt, :, :], b, kt == 0, kt == LT - 1)
                        if j == 1:
                            mm.then_inc(bank_full, 1)
                    if j == 0:
                        mm.then_inc(piece_used, 1)

            def weighted_values(t, s, w):
                h = slice(t * P, (t + 1) * P)
                open_bank(s)
                nc.tensor.matmul(bank_of(s)[:, 0:SEQ], val[:, 0, h], w[:, 0:SEQ], start=True, stop=False)
                nc.tensor.matmul(bank_of(s)[:, P:SEQ], val[:, 1, h], w[:, SEQ:3 * P], start=False,
                                 stop=True).then_inc(bank_full, 1)

            pe.wait_ge(bank_free, BANK_END["kv_mla"])
            pe.wait_ge(rms_applied, 1)
            pe.wait_ge(rope_ready, 1 + HEADS // 2)
            for step in range(HEADS + 2):
                if step < HEADS:
                    t = step
                    s = MLA_BANK["scores", t]
                    open_bank(s)
                    r = slice(ROPE * (t % 2), ROPE * (t % 2) + ROPE)
                    for q, (c0, keys) in enumerate(((0, P), (P, 2 * P))):
                        qs = slice(q * P, (q + 1) * P)
                        dst = bank_of(s)[:, c0:c0 + keys]
                        nc.tensor.matmul(dst, queryT[:, t, qs], keyT[:, t, 0:keys], start=True, stop=False)
                        mm = nc.tensor.matmul(dst, qropeT[r, t // 2, qs], kropeT[r, 0:keys], start=False, stop=True)
                    mm.then_inc(bank_full, 1)
                if step >= 2:
                    t = step - 2
                    pe.wait_ge(bank_free, MLA_BANK["turned", t] + 1)
                    weighted_values(t, MLA_BANK["out", t], probsT[:, t % 2, :])
                fill("mla_out", MLA_BANK, step)
                if 1 <= step <= HEADS:
                    t = step - 1
                    s = MLA_BANK["turned", t]
                    open_bank(s)
                    pe.wait_ge(probs_ready, 2 * t + 2)
                    for j in range(3):
                        mm = nc.tensor.transpose(bank_of(s)[:, j * P:(j + 1) * P],
                                                 probs[:, t % 2, j * P:(j + 1) * P], ident)
                    mm.then_inc(bank_full, 1)
            pe.wait_ge(bank_free, BANK_END["mla"])
            token_unit(2 * CHUNK0["mla_out"], BANK0["mla_out"], first=FILLED)

            def mlp(name, post):
                def one(start, part, ready=None):
                    poff, soff, foff = part * MLP_PIECES, part * MLP_BANKS, part * FEATURE_BANKS
                    p0, s0 = 2 * CHUNK0[name] + start * MLP_PIECES, BANK0[name] + start * MLP_BANKS
                    feature_unit(p0, s0, poff, soff, ready=ready)

                    def hidden(kp):
                        pe.wait_ge(hidden_ready, HIDDEN[name] + start * FEATURE_BANKS + 2 * kp + 2 + foff)

                    token_unit(p0 + UNIT_PIECES, s0 + FEATURE_BANKS, poff, soff, op=hidT, ready=hidden)

                one(0, 0, turning("turn_" + name, post))
                with pe.Fori(0, FFN_PARTS - 1) as part:
                    one(1, part)

            mlp("mlp0", "post_mla")
            feature_unit(2 * CHUNK0["k_shared"], BANK0["k_shared"], ready=turning("turn_kv", "post_mlp0"))
            spread_rms("spread_kv", 1)
            token_unit(2 * CHUNK0["v_shared"], BANK0["v_shared"])

            def logits(t):
                s = STICK_BANK["logits", t]
                open_bank(s)
                z = bank_of(s)
                pe.wait_ge(rms_applied, QUERY_SCALED + t + 1)
                nc.tensor.matmul(z[:, 0:SEQ], keyT[:, t, 0:P], queryT[:, t, :], start=True, stop=False,
                                 skip_group_check=True)
                nc.tensor.matmul(z[:, SEQ:3 * P], keyT[:, t, P:SEQ], queryT[:, t, P:SEQ], start=False,
                                 stop=False, skip_group_check=True).then_inc(logit_ready, 1)

            feature_unit(2 * CHUNK0["q_stick"], BANK0["q_stick"], ready=turning("turn_q"),
                         before_last=lambda: logits(0))

            suffix, later = con[:, SUFFIX:SUFFIX + P], con[:, LATER:LATER + P]
            for step in range(HEADS + 2):
                if 1 <= step < HEADS:
                    logits(step)
                fill("stick_out", STICK_BANK, step)
                if 1 <= step <= HEADS:
                    t = step - 1
                    z, sp_ = bank_of(STICK_BANK["logits", t]), soft[:, 2 + t % 2, :]
                    pe.wait_ge(masked_softplus, t + 1)
                    nc.tensor.matmul(z[:, 0:SEQ], suffix, sp_[:, 0:SEQ], start=False, stop=False,
                                     skip_group_check=True)
                    nc.tensor.matmul(z[:, P:SEQ], later, sp_[:, SEQ:3 * P], start=False, stop=False,
                                     skip_group_check=True)
                    nc.tensor.matmul(z[:, SEQ:3 * P], suffix, sp_[:, SEQ:3 * P], start=False, stop=True,
                                     skip_group_check=True).then_inc(bank_full, 1)
                if step >= 2:
                    t = step - 2
                    pe.wait_ge(stick_ready, t + 1)
                    weighted_values(t, STICK_BANK["out", t], probs[:, t % 2, :])
            pe.wait_ge(bank_free, BANK_END["stick"])
            token_unit(2 * CHUNK0["stick_out"], BANK0["stick_out"], first=FILLED)
            mlp("mlp1", "post_stick")

        @block.vector
        def _(dve):
            def split_lo(p, part=0):
                dve.wait_ge(hi_ready, p + 1 + part * MLP_PIECES)
                moves = split_moves(p)
                for src, hi, lo in moves[:-1]:
                    nc.vector.tensor_tensor(lo, src, hi.bitcast(F32), ALU.subtract)
                src, hi, lo = moves[-1]
                nc.vector.tensor_tensor(lo, src, hi.bitcast(F32), ALU.subtract).then_inc(lo_ready, 1)

            def split_ahead(p, part=0):
                if p + PIECE_SLOTS < PIECES:
                    split_lo(p + PIECE_SLOTS, part)

            def add_halves(dst, s, off, i, half, scale=1.0):
                dve.wait_ge(half_ready, half + 1)
                nc.vector.scalar_tensor_tensor(out=dst, in0=bank_of(s)[:, 0:SEQ], scalar=scale,
                                               in1=half_sum[:, i % 4, :], op0=ALU.mult,
                                               op1=ALU.add).then_inc(bank_free, 1)

            def swap_rope(s, n):
                dve.wait_ge(bank_free, s + 1)
                for q in (0, 1):
                    src = full_sum[32 * (q ^ 1):32 * (q ^ 1) + 32, 2 * (n % 2), :]
                    nc.vector.tensor_copy(full_sum[32 * q:32 * q + 32, 2 * (n % 2) + 1, :],
                                          src).then_inc(swapped_low, 1)

            def sum_parts(name):
                r, i = REQUEST[name], STAT[name]
                _, cols, parts = NORMS[r]
                dve.wait_ge(squares_ready, SQUARES[name] + cols * parts)
                nc.vector.tensor_reduce(stat[:, 0, i:i + cols], squares[:, i:i + cols, 0:parts], AX_X,
                                        ALU.add).then_inc(sum_ready, 1)

            def scale_last(name, b):
                g = QUARTERS - 1
                last = branch[:, b, g * NCOL:(g + 1) * NCOL]
                dve.wait_ge(post_gain_loaded, 16 * POST_GAIN_LOADS[name])
                dve.wait_ge(squares_ready, SQUARES[name] + TB * g + b + 1)
                if b == TB - 1:
                    sum_parts(name)
                nc.vector.tensor_tensor(last, last, gain_post[:, g * NCOL:(g + 1) * NCOL],
                                        ALU.mult).then_inc(last_scaled, 1)

            def branch_ready(name):
                scale_last(name, TB - 1)
                dve.wait_ge(gain_scaled, GAINED[name] + (QUARTERS - 1) * TB)
                dve.wait_ge(rms_ready, REQUEST[name] + 1)
                dve.wait_ge(last_scaled, TB * POST_GAIN_LOADS[name])

            def add_branch(name, q):
                cols = slice(q * NCOL, (q + 1) * NCOL)
                for b in range(TB):
                    i = STAT[name] + b
                    nc.vector.scalar_tensor_tensor(out=resid[:, b, cols], in0=branch[:, b, cols],
                                                   scalar=stat[:, 2, i:i + 1], in1=resid[:, b, cols],
                                                   op0=ALU.mult, op1=ALU.add).then_inc(resid_ready, 1)

            def turn_lo(name, i, k0=0):
                s = BANK0[name] + i
                dve.wait_ge(turned_hi, TURN[name] + i + 1)
                if name not in PRE_GAINS:
                    k = slice(k0 + 2 * i, k0 + 2 * i + 2)
                    nc.vector.tensor_tensor(xT[:, k, 1, :], bank_of(s).rearrange("p (k t) -> p k t", k=2),
                                            xT[:, k, 0, :].bitcast(F32), ALU.subtract).then_inc(bank_free, 1)
                    return
                g = PRE_GAINS.index(name) * KT
                for k, last in ((2 * i, False), (2 * i + 1, True)):
                    rest = nc.vector.scalar_tensor_tensor(
                        out=xT[:, k, 1, :], in0=bank_of(s)[:, (k % 2) * SEQ:(k % 2 + 1) * SEQ],
                        scalar=gainT[:, g + k:g + k + 1], in1=xT[:, k, 0, :].bitcast(F32),
                        op0=ALU.mult, op1=ALU.subtract)
                    if last:
                        rest.then_inc(bank_free, 1)

            def turn_stage(name, p0, post=None, pre=None):
                if post:
                    branch_ready(post)
                    add_branch(post, 0)
                    add_branch(post, 1)
                for i in range(TURN_BANKS):
                    if post and i in (1, 2):
                        add_branch(post, i + 1)
                    if i == 2:
                        split_ahead(p0 - 1)
                    if i >= TURN_BANKS - 2:
                        split_ahead(p0 + i - (TURN_BANKS - 2))
                    turn_lo(name, i)
                if pre:
                    sum_parts(pre)

            def feature_stage(name, dst, scale=1.0, first=0, before_last=None):
                for i in range(first, UNIT_PIECES):
                    if before_last and i == UNIT_PIECES - 1:
                        before_last()
                    if i % GROUP_PIECES == GROUP_PIECES - 1:
                        for f in range(4):
                            k = i // GROUP_PIECES * 4 + f
                            add_halves(dst[:, k, :], BANK0[name] + k, 0, f, HALF[name] + k, scale)
                    split_ahead(2 * CHUNK0[name] + i)

            def fill_ahead(name, step):
                k = (step - FILL_LAG - 2) // 2
                if step % 2 == 0 and k >= 0:
                    split_ahead(2 * CHUNK0[name] + k)

            def token_stage(name, dst, groups=D // NCOL, hold=False, first=0, rms_of=None, post=None,
                            sums=None):
                end = groups * GROUP_PIECES

                def take(g, b):
                    s = BANK0[name] + TB * g + b
                    to = latents[g][:, b, :] if dst is None else dst[:, b, g * NCOL:(g + 1) * NCOL]
                    dve.wait_ge(bank_full, s + 1)
                    if rms_of:
                        r = STAT[rms_of] + b
                        dve.wait_ge(rms_ready, REQUEST[rms_of] + 1)
                        nc.vector.tensor_scalar(to, bank_of(s), stat[:, 2, r:r + 1], None,
                                                ALU.mult).then_inc(bank_free, 1)
                    else:
                        nc.vector.tensor_copy(to, bank_of(s)).then_inc(bank_free, 1)

                for i in range(first, end):
                    g = i // GROUP_PIECES
                    if i % GROUP_PIECES == GROUP_PIECES - 1:
                        for b in range(TB):
                            take(g, b)
                    if post and i == UNIT_PIECES - 1:
                        scale_last(post, 0)
                    if not hold or i < UNIT_PIECES - 1:
                        split_ahead(2 * CHUNK0[name] + i)
                    if sums and i == 2 * TB:
                        sum_parts(sums[0])
                    if sums and i == GROUP_PIECES + 2:
                        dve.wait_ge(latent_gain_loaded, 16 * 2)
                        norm_latent(sums[1], 0)

            dve.wait_ge(bank_full, BANK_END["turn_gains"])
            nc.vector.tensor_copy(gainT[:, :], bank_of(BANK0["turn_gains"])[:, 0:len(PRE_GAINS) * KT]).then_inc(bank_free, 1)
            dve.wait_ge(bank_free, BANK_END["turn_gains"])
            for i in range(TURN_BANKS):
                turn_lo("turn_mla", i)
                if i in FIRST_SPLITS:
                    split_lo(FIRST_SPLITS.index(i))

            def norm_latent(name, g):
                sum_parts(name)
                dve.wait_ge(rms_ready, REQUEST[name] + 1)
                for b in range(TB):
                    i = STAT[name] + b
                    c = latents[g][:, b, :]
                    nc.vector.scalar_tensor_tensor(out=c, in0=c, scalar=stat[:, 2, i:i + 1],
                                                   in1=gain_latent[:, g * LORA:(g + 1) * LORA],
                                                   op0=ALU.mult, op1=ALU.mult).then_inc(latent_normed, 1)

            token_stage("latents", None, groups=2, rms_of="pre_mla", sums=["pre_mla", "q_latent"])

            def copy_spread(name):
                s = BANK0[name]
                dve.wait_ge(bank_full, s + 1)
                nc.vector.tensor_copy(spread[:, :], bank_of(s)[:, 0:SEQ]).then_inc(bank_free, 1)

            copy_spread("spread_mla")
            add_halves(full_sum[:, 0, :], BANK0["k_rope"], 0, 0, HALF["k_rope"])
            swap_rope(BANK0["k_rope"], 0)
            for i in range(LT // 2):
                turn_lo("turn_q_latent", i, CQ)
            for i in range(2):
                split_ahead(2 * CHUNK0["k_rope"] + i)
            for i in range(HEADS // 2):
                s, h = q_bank(i), HALF["q_mla"] + 3 * i
                split_ahead(2 * (CHUNK0["q_mla"] + i))
                for f in range(2):
                    add_halves(queryT[:, 2 * i + f, :], s + f, 0, f, h + f, MLA_SCALE)
                n = 1 + i
                if n >= 2:
                    dve.wait_ge(rope_ready, n - 1)
                add_halves(full_sum[:, 2 * (n % 2), :], s + 2, 0, 2, h + 2, MLA_SCALE)
                split_ahead(2 * (CHUNK0["q_mla"] + i) + 1)
                swap_rope(s + 2, n)
                if i == 0:
                    norm_latent("kv_latent", 1)
                if i == 1:
                    for j in range(LT // 2):
                        turn_lo("turn_kv_latent", j, CKV)
            for i in range(HEADS // 2):
                s, h = BANK0["kv_mla"] + 4 * i, HALF["kv_mla"] + 2 * i
                split_ahead(2 * (CHUNK0["kv_mla"] + i))
                for f in range(2):
                    add_halves(keyT[:, 2 * i + f, :], s + f, 0, f, h + f)
                for b in range(TB):
                    dve.wait_ge(bank_full, s + 3 + b)
                    nc.vector.tensor_copy(val[:, b, 2 * i * P:2 * (i + 1) * P],
                                          bank_of(s + 2 + b)[:, 0:2 * P]).then_inc(bank_free, 1)
                split_ahead(2 * (CHUNK0["kv_mla"] + i) + 1)

            def out_rest(t, s, n):
                dve.wait_ge(out_hi, n + 1)
                nc.vector.tensor_tensor(xT[:, t, 1, :], bank_of(s)[:, 0:SEQ], xT[:, t, 0, :].bitcast(F32),
                                        ALU.subtract).then_inc(bank_free, 1)

            for step in range(HEADS + 2):
                if 1 <= step <= HEADS:
                    t = step - 1
                    dve.wait_ge(exp_ready, 2 * t + 2)
                    nc.vector.reciprocal(rows[:, 2, 2 * t:2 * t + 2],
                                         rows[:, 1, 2 * t:2 * t + 2]).then_inc(sum_inverse, 1)
                if step < HEADS:
                    t = step
                    s = MLA_BANK["scores", t]
                    pr = probs[:, t % 2, :]
                    dve.wait_ge(bank_full, s + 1)
                    nc.vector.tensor_tensor(pr, bank_of(s)[:, 0:3 * P], con[:, CAUSAL:CAUSAL + 3 * P],
                                            ALU.add).then_inc(bank_free, 1)
                    dve.wait_ge(bank_free, s + 1)
                    for q, (c0, c1) in enumerate(((0, P), (P, 3 * P))):
                        nc.vector.tensor_reduce(rows[:, 0, 2 * t + q:2 * t + q + 1], pr[:, c0:c1], AX_X,
                                                ALU.max, negate=True).then_inc(row_max, 1)
                if step >= 2:
                    out_rest(step - 2, MLA_BANK["out", step - 2], step - 2)
                if 1 <= step <= HEADS:
                    t = step - 1
                    s = MLA_BANK["turned", t]
                    dve.wait_ge(bank_full, s + 1)
                    nc.vector.tensor_copy(probsT[:, t % 2, :], bank_of(s)[:, 0:3 * P]).then_inc(bank_free, 1)
                fill_ahead("mla_out", step)
            token_stage("mla_out", branch, hold=True, post="post_mla", first=FILLED - 1)
            turn_stage("turn_mlp0", 2 * CHUNK0["mlp0"], "post_mla", "pre_mlp0")

            def mlp_part(name, part, norm=None, last=False, first=0):
                p0, s0 = 2 * CHUNK0[name], BANK0[name]
                soff, foff = part * MLP_BANKS, part * FEATURE_BANKS
                for i in range(first, UNIT_PIECES):
                    if i % GROUP_PIECES == GROUP_PIECES - 1:
                        g = i // GROUP_PIECES
                        for f in range(5):
                            if f < 4:
                                k = 4 * g + f
                                v = full_sum[:, f, :]
                                if k >= 4:
                                    dve.wait_ge(hidden_ready, HIDDEN[name] + k - 3 + foff)
                                add_halves(v, s0 + k, soff, f, HALF[name] + k + foff)
                                dve.wait_ge(bank_free, s0 + k + 1 + soff)
                                nc.vector.scalar_tensor_tensor(out=v, in0=v, scalar=0.0, in1=v, op0=ALU.max,
                                                               op1=ALU.mult).then_inc(relu2_ready, 1)
                            if f >= 1:
                                k = 4 * g + f - 1
                                dve.wait_ge(hidden_hi, HIDDEN[name] + k + 1 + foff)
                                nc.vector.tensor_tensor(hidT[:, k, 1, :], full_sum[:, f - 1, :],
                                                        hidT[:, k, 0, :].bitcast(F32),
                                                        ALU.subtract).then_inc(hidden_ready, 1)
                    split_ahead(p0 + i, part)
                def take(g, b):
                    s = s0 + FEATURE_BANKS + TB * g + b
                    dst = branch[:, b, g * NCOL:(g + 1) * NCOL]
                    r = STAT["pre_" + name] + b
                    dve.wait_ge(bank_full, s + 1 + soff)
                    nc.vector.scalar_tensor_tensor(out=dst, in0=bank_of(s), scalar=stat[:, 3, r:r + 1],
                                                   in1=dst, op0=ALU.mult, op1=ALU.add).then_inc(bank_free, 1)

                for i in range(UNIT_PIECES):
                    g = i // GROUP_PIECES
                    if i % GROUP_PIECES == GROUP_PIECES - 1:
                        for b in range(TB):
                            take(g, b)
                    if norm and i == UNIT_PIECES - 1:
                        scale_last(norm, 0)
                    if i < UNIT_PIECES - (PIECE_SLOTS if last else 1 if norm else 0):
                        split_ahead(p0 + UNIT_PIECES + i, part)

            dve.wait_ge(branch_zeroed, ZEROED["mlp0"])
            dve.wait_ge(square_ready, 1)
            mlp_part("mlp0", 0, first=2)
            with dve.Fori(1, FFN_PARTS - 1) as part:
                mlp_part("mlp0", part)
            mlp_part("mlp0", FFN_PARTS - 1, "post_mlp0")
            turn_stage("turn_kv", 2 * CHUNK0["k_shared"], "post_mlp0", "pre_kv")
            feature_stage("k_shared", keyT, first=2)
            dve.wait_ge(rms_applied, 1)
            copy_spread("spread_kv")
            token_stage("v_shared", val, hold=True, rms_of="pre_kv")
            turn_stage("turn_q", 2 * CHUNK0["q_stick"])

            def masked_terms(t):
                s = STICK_BANK["logits", t]
                spt = soft[:, 2 + t % 2, :]
                dve.wait_ge(log_term, t + 1)
                nc.vector.scalar_tensor_tensor(out=spt, in0=bank_of(s)[:, 0:3 * P], scalar=0.0,
                                               in1=soft[:, t % 2, :], op0=ALU.max,
                                               op1=ALU.add).then_inc(softplus, 1)
                diag = spt.rearrange("p (b n) -> p b n", b=3)[:, 0:3:2, :]
                dve.wait_ge(softplus, t + 1)
                nc.vector.tensor_tensor(diag, diag, strict2, ALU.mult).then_inc(masked_softplus, 1)

            feature_stage("q_stick", queryT, STICK_SCALE, first=2, before_last=lambda: masked_terms(0))

            dve.wait_ge(bank_free, BANK_END["q_stick"])
            for step in range(HEADS + 2):
                if 1 <= step <= HEADS:
                    t = step - 1
                    s = STICK_BANK["logits", t]
                    dve.wait_ge(bank_full, s + 1)
                    nc.vector.tensor_scalar(probs[:, t % 2, :], bank_of(s)[:, 0:3 * P], 0.0, None,
                                            ALU.min).then_inc(bank_free, 1)
                if 1 <= step < HEADS:
                    masked_terms(step)
                if step >= 2:
                    out_rest(step - 2, STICK_BANK["out", step - 2], HEADS + step - 2)
                fill_ahead("stick_out", step)
            token_stage("stick_out", branch, hold=True, post="post_stick", first=FILLED - 1)
            turn_stage("turn_mlp1", 2 * CHUNK0["mlp1"], "post_stick", "pre_mlp1")
            dve.wait_ge(branch_zeroed, ZEROED["mlp1"])
            dve.wait_ge(square_ready, 2)
            mlp_part("mlp1", 0, first=2)
            with dve.Fori(1, FFN_PARTS - 1) as part:
                mlp_part("mlp1", part)
            mlp_part("mlp1", FFN_PARTS - 1, "post_mlp1", last=True)
            branch_ready("post_mlp1")
            for q in range(QUARTERS):
                add_branch("post_mlp1", q)


_INS = ["x", "a_pre_g", "a_post_g", "a_w_dq_dkv", "a_q_norm_g", "a_kv_norm_g", "a_w_uq", "a_w_ukv",
        "a_w_o", "kv_norm_g", "w_kv_shared", "b_pre_g", "b_post_g", "b_w_q", "b_w_o", "mlp_pre_g",
        "mlp_post_g", "mlp_w_up", "mlp_w_down"]


def kernel(**inputs):
    import concourse.bacc as _bacc
    from concourse.bass_utils import run_bass_kernel_spmd as _run

    nc = _bacc.Bacc("TRN2", target_bir_lowering=False, num_devices=1)
    arrays, args = {}, []
    for name in _INS:
        a = np.ascontiguousarray(inputs[name])
        arrays[f"in_{name}"] = a
        args.append(nc.dram_tensor(f"in_{name}", a.shape, mybir.dt.from_np(a.dtype), kind="ExternalInput").ap())
    c = shape_constants()
    arrays["shape_constants"] = c
    args.append(nc.dram_tensor("shape_constants", c.shape, F32, kind="ExternalInput").ap())
    args.append(nc.dram_tensor("out", (1, SEQ, D), F32, kind="ExternalOutput").ap())
    trunk(nc, *args)
    r = _run(nc, [arrays], core_ids=[0])
    return r.results[0]["out"]
```
